# Optimizing a Trainium2 kernel written in Bass

```python
import math
import jax, jax.numpy as jnp
from jax import lax
import numpy as np

D_MODEL = 1024
BATCH = 1
SEQ = 512
DEPTH = 1

HEAD_DIM = 64
A_HEADS = 4
A_VDIM = 2 * HEAD_DIM
B_HEADS = 8
B_KV_HEADS = 2
B_WINDOW = 128
C_HEADS = 8
C_KV_HEADS = 2
CMP_BLOCK = 32
CMP_STRIDE = 16
CMP_HIDDEN = 256
SEL_BLOCK = 64
N_SELECT = 16
C_WINDOW = 512
MIX_WIDTH = B_HEADS * HEAD_DIM
N_BRANCH = 3
D_FF = 4 * D_MODEL
NUM_BUCKETS = 32
MAX_DISTANCE = 128
TOTAL_HEADS = A_HEADS + B_HEADS + C_HEADS
Q_BLOCK = 128
SEL_Q_BLOCK = 64
NEG_INF = -1e30
FORCE_BONUS = 1e4
EPS = 1e-6

SPLIT_SIZES = (
    A_HEADS * 2 * HEAD_DIM,
    A_HEADS * 2 * HEAD_DIM,
    A_HEADS * A_VDIM,
    B_HEADS * HEAD_DIM,
    B_KV_HEADS * HEAD_DIM,
    B_KV_HEADS * HEAD_DIM,
    C_HEADS * HEAD_DIM,
    6 * C_KV_HEADS * HEAD_DIM,
    C_HEADS * 3,
    N_BRANCH * D_MODEL,
)
IN_COLS = sum(SPLIT_SIZES)


def rms_norm(x, g):
    xf = x.astype(jnp.float32)
    y = xf * lax.rsqrt(jnp.mean(xf * xf, axis=-1, keepdims=True) + EPS)
    return (y * g.astype(jnp.float32)).astype(x.dtype)

def rel_bucket(dist):
    n = jnp.maximum(dist, 0)
    max_exact = NUM_BUCKETS // 2
    nf = jnp.maximum(n, 1).astype(jnp.float32)
    large = max_exact + (jnp.log(nf / max_exact) / math.log(MAX_DISTANCE / max_exact)
                         * (NUM_BUCKETS - max_exact)).astype(jnp.int32)
    large = jnp.minimum(large, NUM_BUCKETS - 1)
    return jnp.where(n < max_exact, n, large)

def diff_attention(q, k, v, lam, bias_tab):
    B, S, H, _, D = q.shape
    nb = S // Q_BLOCK
    scale = D ** -0.5
    k_pos = jnp.arange(S)
    qb = q.reshape(B, nb, Q_BLOCK, H, 2, D).transpose(1, 0, 2, 3, 4, 5)

    def block(args):
        i, qi = args
        q_pos = i * Q_BLOCK + jnp.arange(Q_BLOCK)
        dist = q_pos[:, None] - k_pos[None, :]
        mask = dist >= 0
        bias = bias_tab[rel_bucket(dist)].transpose(2, 0, 1).astype(jnp.float32)
        s = jnp.einsum('bqhcd,bkhcd->cbhqk', qi, k).astype(jnp.float32) * scale + bias
        p = jax.nn.softmax(jnp.where(mask, s, NEG_INF), axis=-1)
        w = p[0] - lam * p[1]
        return jnp.einsum('bhqk,bkhe->bqhe', w.astype(v.dtype), v)

    out = lax.map(block, (jnp.arange(nb), qb))
    return out.transpose(1, 0, 2, 3, 4).reshape(B, S, H, v.shape[-1])

def banded_attention(q, k, v, bias_tab, window, sink=None):
    B, S, H, D = q.shape
    G = k.shape[2]
    R = H // G
    nb = S // Q_BLOCK
    n_prev = -(-window // Q_BLOCK)
    kw = (n_prev + 1) * Q_BLOCK

    def band(t):
        tb = t.reshape(B, nb, Q_BLOCK, G, D)
        tb = jnp.pad(tb, ((0, 0), (n_prev, 0), (0, 0), (0, 0), (0, 0)))
        return jnp.concatenate([tb[:, j:j + nb] for j in range(n_prev + 1)], axis=2)

    kb, vb = band(k), band(v)
    qb = q.reshape(B, nb, Q_BLOCK, G, R, D)
    r = jnp.arange(Q_BLOCK)
    c = jnp.arange(kw)
    dist = n_prev * Q_BLOCK + r[:, None] - c[None, :]
    k_pos = (jnp.arange(nb)[:, None] - n_prev) * Q_BLOCK + c[None, :]
    mask = ((dist >= 0) & (dist < window))[None] & (k_pos >= 0)[:, None, :]
    bias = bias_tab[rel_bucket(dist)].reshape(Q_BLOCK, kw, G, R).transpose(2, 3, 0, 1).astype(jnp.float32)
    s = jnp.einsum('bnqgrd,bnkgd->bngrqk', qb, kb).astype(jnp.float32) * D ** -0.5 + bias
    s = jnp.where(mask[:, None, None], s, NEG_INF)
    if sink is None:
        p = jax.nn.softmax(s, axis=-1)
    else:
        sk = sink.astype(jnp.float32).reshape(G, R, 1, 1)
        m = jnp.maximum(jnp.max(s, axis=-1, keepdims=True), sk)
        e = jnp.exp(s - m)
        p = e / (jnp.sum(e, axis=-1, keepdims=True) + jnp.exp(sk - m))
    o = jnp.einsum('bngrqk,bnkgd->bnqgrd', p.astype(v.dtype), vb)
    return o.reshape(B, S, H, D)

def compress_blocks(t, pos, w1, w2):
    B, S, G, D = t.shape
    nc = (S - CMP_BLOCK) // CMP_STRIDE + 1
    idx = jnp.arange(nc)[:, None] * CMP_STRIDE + jnp.arange(CMP_BLOCK)[None, :]
    blocks = t[:, idx] + pos[None, None, :, None, :]
    flat = blocks.transpose(0, 1, 3, 2, 4).reshape(B, nc, G, CMP_BLOCK * D)
    return jax.nn.gelu(flat @ w1) @ w2

def nsa_attention(q, kc, vc, ks, vs, kw, vw, gates, bias_tab):
    B, S, H, D = q.shape
    G = ks.shape[2]
    R = H // G
    nc = kc.shape[1]
    scale = D ** -0.5
    qg = q.reshape(B, S, G, R, D)
    t_pos = jnp.arange(S)

    c_start = jnp.arange(nc) * CMP_STRIDE
    cmask = (c_start + CMP_BLOCK - 1)[None, :] <= t_pos[:, None]
    s = jnp.einsum('bsgrd,bcgd->bgrsc', qg, kc).astype(jnp.float32) * scale
    p_cmp = jnp.where(cmask, jax.nn.softmax(jnp.where(cmask, s, NEG_INF), axis=-1), 0.0)
    o_cmp = jnp.einsum('bgrsc,bcgd->bsgrd', p_cmp.astype(vc.dtype), vc).reshape(B, S, H, D)

    n_blk = S // SEL_BLOCK
    j_start = jnp.arange(n_blk) * SEL_BLOCK
    overlap = ((c_start[:, None] < j_start[None, :] + SEL_BLOCK)
               & (c_start[:, None] + CMP_BLOCK > j_start[None, :])).astype(jnp.float32)
    imp = jnp.einsum('bgrsc,cj->bgsj', p_cmp, overlap)
    cur = t_pos // SEL_BLOCK
    jj = jnp.arange(n_blk)
    valid = j_start[None, :] <= t_pos[:, None]
    forced = (jj[None, :] == 0) | (jj[None, :] == cur[:, None]) | (jj[None, :] == cur[:, None] - 1)
    score = jnp.where(valid, imp + jnp.where(forced, FORCE_BONUS, 0.0), NEG_INF)
    n_sel = min(N_SELECT, n_blk)
    _, sel_idx = lax.top_k(score, n_sel)

    kbk = ks.reshape(B, n_blk, SEL_BLOCK, G, D).transpose(0, 3, 1, 2, 4)
    vbk = vs.reshape(B, n_blk, SEL_BLOCK, G, D).transpose(0, 3, 1, 2, 4)
    nqb = S // SEL_Q_BLOCK
    qs = qg.reshape(B, nqb, SEL_Q_BLOCK, G, R, D).transpose(1, 0, 2, 3, 4, 5)
    idx_b = sel_idx.reshape(B, G, nqb, SEL_Q_BLOCK, n_sel).transpose(2, 0, 1, 3, 4)
    bi = jnp.arange(B)[:, None, None, None]
    gi = jnp.arange(G)[None, :, None, None]
    bias_g = bias_tab.reshape(NUM_BUCKETS, G, R).transpose(1, 0, 2)

    def sel_block(args):
        i, qi, ii = args
        kg = kbk[bi, gi, ii]
        vg = vbk[bi, gi, ii].reshape(B, G, SEL_Q_BLOCK, n_sel * SEL_BLOCK, D)
        q_pos = i * SEL_Q_BLOCK + jnp.arange(SEL_Q_BLOCK)
        k_pos = (ii[..., None] * SEL_BLOCK + jnp.arange(SEL_BLOCK)).reshape(B, G, SEL_Q_BLOCK, n_sel * SEL_BLOCK)
        dist = q_pos[None, None, :, None] - k_pos
        mask = dist >= 0
        bias = bias_g[gi, rel_bucket(dist)].transpose(0, 1, 4, 2, 3).astype(jnp.float32)
        s = jnp.einsum('bqgrd,bgqnkd->bgrqnk', qi, kg).reshape(B, G, R, SEL_Q_BLOCK, n_sel * SEL_BLOCK)
        s = s.astype(jnp.float32) * scale + bias
        p = jax.nn.softmax(jnp.where(mask[:, :, None], s, NEG_INF), axis=-1)
        return jnp.einsum('bgrqk,bgqkd->bqgrd', p.astype(vg.dtype), vg)

    o_sel = lax.map(sel_block, (jnp.arange(nqb), qs, idx_b))
    o_sel = o_sel.transpose(1, 0, 2, 3, 4, 5).reshape(B, S, H, D)

    o_win = banded_attention(q, kw, vw, bias_tab, C_WINDOW)

    g = jax.nn.sigmoid(gates.astype(jnp.float32)).astype(q.dtype)
    out = g[..., 0:1] * o_cmp + g[..., 1:2] * o_sel + g[..., 2:3] * o_win
    return out.reshape(B, S, H * D)

def first_inputs(seed: int = 0) -> dict:
    key = jax.random.key(seed)
    ks = jax.random.split(key, 17)

    def nrm(k, shape, scale):
        return jax.random.normal(k, shape, jnp.float32) * scale

    return {
        'x': nrm(ks[0], (BATCH, SEQ, D_MODEL), 1.0),
        'w_in': nrm(ks[1], (DEPTH, D_MODEL, IN_COLS), D_MODEL ** -0.5),
        'qk_gain': 1.0 + nrm(ks[2], (DEPTH, 8, HEAD_DIM), 0.1),
        'diff_lambda': nrm(ks[3], (DEPTH, 4, HEAD_DIM), 0.1),
        'diff_subln': 1.0 + nrm(ks[4], (DEPTH, A_VDIM), 0.1),
        'sinks': nrm(ks[5], (DEPTH, B_HEADS), 0.5),
        'cmp_pos': nrm(ks[6], (DEPTH, 2, CMP_BLOCK, HEAD_DIM), 0.5),
        'cmp_w1': nrm(ks[7], (DEPTH, 2, CMP_BLOCK * HEAD_DIM, CMP_HIDDEN), (CMP_BLOCK * HEAD_DIM) ** -0.5),
        'cmp_w2': nrm(ks[8], (DEPTH, 2, CMP_HIDDEN, HEAD_DIM), CMP_HIDDEN ** -0.5),
        'w_branch': nrm(ks[9], (DEPTH, N_BRANCH, MIX_WIDTH, D_MODEL), MIX_WIDTH ** -0.5),
        'w_out': nrm(ks[10], (DEPTH, D_MODEL, D_MODEL), D_MODEL ** -0.5),
        'norm_mix': 1.0 + nrm(ks[11], (DEPTH, D_MODEL), 0.1),
        'norm_mlp': 1.0 + nrm(ks[12], (DEPTH, D_MODEL), 0.1),
        'w_up': nrm(ks[13], (DEPTH, D_MODEL, D_FF), D_MODEL ** -0.5),
        'w_down': nrm(ks[14], (DEPTH, D_FF, D_MODEL), D_FF ** -0.5),
        'rel_bias': nrm(ks[15], (NUM_BUCKETS, TOTAL_HEADS), 0.5),
    }

def first_block(x, w_in, qk_gain, diff_lambda, diff_subln, sinks, cmp_pos, cmp_w1, cmp_w2,
              w_branch, w_out, norm_mix, norm_mlp, w_up, w_down, rel_bias):
    B, S, _ = x.shape
    points = []
    acc = 0
    for size in SPLIT_SIZES[:-1]:
        acc += size
        points.append(acc)
    bias_a = rel_bias[:, :A_HEADS]
    bias_b = rel_bias[:, A_HEADS:A_HEADS + B_HEADS]
    bias_c = rel_bias[:, A_HEADS + B_HEADS:]

    for layer in range(DEPTH):
        h = rms_norm(x, norm_mix[layer])
        proj = h @ w_in[layer]
        aq, ak, av, bq, bk, bv, cq, ckv, cg, mg = jnp.split(proj, points, axis=-1)
        gains = qk_gain[layer]

        aq = rms_norm(aq.reshape(B, S, A_HEADS, 2, HEAD_DIM), gains[0])
        ak = rms_norm(ak.reshape(B, S, A_HEADS, 2, HEAD_DIM), gains[1])
        av = av.reshape(B, S, A_HEADS, A_VDIM)
        lmb = diff_lambda[layer].astype(jnp.float32)
        lam_init = 0.8 - 0.6 * math.exp(-0.3 * layer)
        lam = jnp.exp(jnp.sum(lmb[0] * lmb[1])) - jnp.exp(jnp.sum(lmb[2] * lmb[3])) + lam_init
        oa = diff_attention(aq, ak, av, lam, bias_a)
        oa = (rms_norm(oa, diff_subln[layer]) * (1.0 - lam_init)).reshape(B, S, MIX_WIDTH)

        bq = rms_norm(bq.reshape(B, S, B_HEADS, HEAD_DIM), gains[2])
        bk = rms_norm(bk.reshape(B, S, B_KV_HEADS, HEAD_DIM), gains[3])
        bv = bv.reshape(B, S, B_KV_HEADS, HEAD_DIM)
        ob = banded_attention(bq, bk, bv, bias_b, B_WINDOW, sinks[layer]).reshape(B, S, MIX_WIDTH)

        cq = rms_norm(cq.reshape(B, S, C_HEADS, HEAD_DIM), gains[4])
        ckv = ckv.reshape(B, S, 6, C_KV_HEADS, HEAD_DIM)
        kc = rms_norm(compress_blocks(ckv[:, :, 0], cmp_pos[layer, 0], cmp_w1[layer, 0], cmp_w2[layer, 0]), gains[5])
        vc = compress_blocks(ckv[:, :, 1], cmp_pos[layer, 1], cmp_w1[layer, 1], cmp_w2[layer, 1])
        ksel = rms_norm(ckv[:, :, 2], gains[6])
        kwin = rms_norm(ckv[:, :, 4], gains[7])
        oc = nsa_attention(cq, kc, vc, ksel, ckv[:, :, 3], kwin, ckv[:, :, 5],
                           cg.reshape(B, S, C_HEADS, 3), bias_c)

        branches = jnp.stack([oa, ob, oc], axis=0)
        y = jnp.einsum('nbsm,nmd->bsnd', branches, w_branch[layer])
        gate = jax.nn.sigmoid(mg.reshape(B, S, N_BRANCH, D_MODEL).astype(jnp.float32)).astype(y.dtype)
        x = x + jnp.sum(gate * y, axis=2) @ w_out[layer]

        h = rms_norm(x, norm_mlp[layer])
        x = x + jnp.square(jax.nn.relu(h @ w_up[layer])) @ w_down[layer]
    return x


DEPTH_2 = 2

CHUNK = 64
LEFT_CHUNKS = 8
BAND = (LEFT_CHUNKS + 1) * CHUNK
N_HEADS_A = 8
N_HEADS_C = 8
WIDTH_A = N_HEADS_A * HEAD_DIM
WIDTH_C = N_HEADS_C * HEAD_DIM
POOL_WINDOWS = (2, 4, 8, 16)
N_POOL_GROUPS = 4
POOL_GROUP_DIM = 128
WIDTH_B = N_POOL_GROUPS * POOL_GROUP_DIM
REL_CLIP = 128
N_REL = 2 * REL_CLIP + 1
N_BRANCHES = 3
D_FF_2 = 2816
N_MOD = 9
NEG_INF_2 = -1e30

SPLIT_SIZES_2 = (WIDTH_A, WIDTH_A, WIDTH_A, WIDTH_B, WIDTH_C, WIDTH_C, WIDTH_C, N_HEADS_C, N_BRANCHES * D_MODEL)
D_IN = sum(SPLIT_SIZES_2)
SPLIT_POINTS = tuple(int(p) for p in np.cumsum(SPLIT_SIZES_2)[:-1])


def rms_norm_2(x, gain):
    xf = x.astype(jnp.float32)
    y = xf * lax.rsqrt(jnp.mean(xf * xf, axis=-1, keepdims=True) + EPS)
    return (y * gain.astype(jnp.float32)).astype(x.dtype)

def modulate(h, shift, scale):
    return h * (1 + scale[:, None, :]) + shift[:, None, :]

def swiglu(h, w_gate, w_up, w_down):
    return (jax.nn.silu(h @ w_gate) * (h @ w_up)) @ w_down

def chunked_relpos_attention(q, k, v, gq, gk, rel_bias):
    B, S, H, dh = q.shape
    nc = S // CHUNK
    qf = rms_norm_2(q, gq).astype(jnp.float32) * (dh ** -0.5)
    kf = rms_norm_2(k, gk).astype(jnp.float32)
    qc = qf.reshape(B, nc, CHUNK, H, dh)
    pad = ((0, 0), (LEFT_CHUNKS * CHUNK, 0), (0, 0), (0, 0))
    kp = jnp.pad(kf, pad).reshape(B, nc + LEFT_CHUNKS, CHUNK, H, dh)
    vp = jnp.pad(v, pad).reshape(B, nc + LEFT_CHUNKS, CHUNK, H, dh)
    band_idx = np.arange(nc)[:, None] + np.arange(LEFT_CHUNKS + 1)[None, :]
    kb = kp[:, band_idx].reshape(B, nc, BAND, H, dh)
    vb = vp[:, band_idx].reshape(B, nc, BAND, H, dh)
    logits = jnp.einsum('bnqhd,bnkhd->bhnqk', qc, kb)
    rel = np.arange(CHUNK)[:, None] + LEFT_CHUNKS * CHUNK - np.arange(BAND)[None, :]
    rel_idx = np.clip(rel, -REL_CLIP, REL_CLIP) + REL_CLIP
    bias = rel_bias[:, rel_idx].astype(jnp.float32)
    valid = np.repeat(band_idx >= LEFT_CHUNKS, CHUNK, axis=1)
    logits = jnp.where(valid[None, None, :, None, :], logits + bias[None, :, None], NEG_INF_2)
    p = jax.nn.softmax(logits, axis=-1).astype(v.dtype)
    out = jnp.einsum('bhnqk,bnkhd->bnqhd', p, vb)
    return out.reshape(B, S, H * dh)

def multiscale_pool(u, w_pool, pool_scale):
    B, S, _ = u.shape
    uf = u.astype(jnp.float32)
    cs = jnp.concatenate([jnp.zeros((B, 1, WIDTH_B), jnp.float32), jnp.cumsum(uf, axis=1)], axis=1)
    t = jnp.arange(S, dtype=jnp.float32)
    diffs = []
    for g, w in enumerate(POOL_WINDOWS):
        sl = slice(g * POOL_GROUP_DIM, (g + 1) * POOL_GROUP_DIM)
        csg = cs[:, :, sl]
        upper = csg[:, 1:]
        lower = jnp.pad(csg[:, :S + 1 - w], ((0, 0), (w - 1, 0), (0, 0)))
        count = jnp.minimum(t + 1, float(w))[None, :, None]
        diffs.append((upper - lower) / count - uf[:, :, sl])
    d = jnp.stack(diffs, axis=2).astype(u.dtype)
    y = jnp.einsum('bsgc,gce->bsge', d, w_pool).reshape(B, S, WIDTH_B)
    return y * pool_scale

def forgetting_attention(q, k, v, gq, gk, f_logit):
    B, S, H, dh = q.shape
    qf = rms_norm_2(q, gq).astype(jnp.float32) * (dh ** -0.5)
    kf = rms_norm_2(k, gk).astype(jnp.float32)
    cum_logf = jnp.cumsum(jax.nn.log_sigmoid(f_logit.astype(jnp.float32)), axis=1)
    cum_k = cum_logf.transpose(0, 2, 1)
    kpos = jnp.arange(S)

    def block(i):
        start = i * Q_BLOCK
        qb = lax.dynamic_slice_in_dim(qf, start, Q_BLOCK, axis=1)
        cq = lax.dynamic_slice_in_dim(cum_k, start, Q_BLOCK, axis=2)
        logits = jnp.einsum('bqhd,bkhd->bhqk', qb, kf) + (cq[..., None] - cum_k[:, :, None, :])
        qpos = start + jnp.arange(Q_BLOCK)
        mask = kpos[None, :] <= qpos[:, None]
        logits = jnp.where(mask[None, None], logits, NEG_INF_2)
        p = jax.nn.softmax(logits, axis=-1).astype(v.dtype)
        return jnp.einsum('bhqk,bkhd->bqhd', p, v)

    out = lax.map(block, jnp.arange(S // Q_BLOCK))
    return out.transpose(1, 0, 2, 3, 4).reshape(B, S, H * dh)

def hybrid_mixer(h, w_in, qk_gain, rel_bias, forget_bias, w_pool, pool_scale, w_branch, w_out):
    B, S, _ = h.shape
    proj = h @ w_in
    qa, ka, va, ub, qc, kc, vc, f_lin, g_lin = jnp.split(proj, SPLIT_POINTS, axis=-1)
    ha = lambda t: t.reshape(B, S, N_HEADS_A, HEAD_DIM)
    hc = lambda t: t.reshape(B, S, N_HEADS_C, HEAD_DIM)
    ya = chunked_relpos_attention(ha(qa), ha(ka), ha(va), qk_gain[0], qk_gain[1], rel_bias)
    yb = multiscale_pool(ub, w_pool, pool_scale)
    yc = forgetting_attention(hc(qc), hc(kc), hc(vc), qk_gain[2], qk_gain[3], f_lin + forget_bias)
    ys = jnp.stack([ya, yb, yc], axis=2)
    branch = jnp.einsum('bsnw,nwd->bsnd', ys, w_branch)
    gates = jax.nn.sigmoid(g_lin.reshape(B, S, N_BRANCHES, D_MODEL))
    merged = jnp.sum(gates * branch, axis=2)
    return merged @ w_out

def second_inputs(seed: int = 0) -> dict:
    key = jax.random.key(seed)
    ks = jax.random.split(key, 18)
    nrm = lambda k, shape, s: jax.random.normal(k, shape, jnp.float32) * s
    return {
        "x": nrm(ks[0], (BATCH, SEQ, D_MODEL), 1.0),
        "c": nrm(ks[1], (BATCH, D_MODEL), 1.0),
        "w_ada": nrm(ks[2], (DEPTH_2, D_MODEL, N_MOD * D_MODEL), 0.5 * D_MODEL ** -0.5),
        "b_ada": nrm(ks[3], (DEPTH_2, N_MOD * D_MODEL), 0.02),
        "norm_gain": 1.0 + nrm(ks[4], (DEPTH_2, 3, D_MODEL), 0.05),
        "ffn_w_gate": nrm(ks[5], (DEPTH_2, 2, D_MODEL, D_FF_2), D_MODEL ** -0.5),
        "ffn_w_up": nrm(ks[6], (DEPTH_2, 2, D_MODEL, D_FF_2), D_MODEL ** -0.5),
        "ffn_w_down": nrm(ks[7], (DEPTH_2, 2, D_FF_2, D_MODEL), D_FF_2 ** -0.5),
        "w_in": nrm(ks[8], (DEPTH_2, D_MODEL, D_IN), D_MODEL ** -0.5),
        "qk_gain": 1.0 + nrm(ks[9], (DEPTH_2, 4, HEAD_DIM), 0.05),
        "rel_bias": nrm(ks[10], (DEPTH_2, N_HEADS_A, N_REL), 0.5),
        "forget_bias": 1.0 + 3.0 * jax.random.uniform(ks[11], (DEPTH_2, N_HEADS_C), jnp.float32),
        "w_pool": nrm(ks[12], (DEPTH_2, N_POOL_GROUPS, POOL_GROUP_DIM, POOL_GROUP_DIM), POOL_GROUP_DIM ** -0.5),
        "pool_scale": 1.0 + nrm(ks[13], (DEPTH_2, WIDTH_B), 0.05),
        "w_branch": nrm(ks[14], (DEPTH_2, N_BRANCHES, WIDTH_A, D_MODEL), WIDTH_A ** -0.5),
        "w_out": nrm(ks[15], (DEPTH_2, D_MODEL, D_MODEL), D_MODEL ** -0.5),
    }

def second_block(x, c, w_ada, b_ada, norm_gain, ffn_w_gate, ffn_w_up, ffn_w_down, w_in, qk_gain,
              rel_bias, forget_bias, w_pool, pool_scale, w_branch, w_out):
    B = x.shape[0]
    c_act = jax.nn.silu(c)
    for l in range(DEPTH_2):
        mod = (c_act @ w_ada[l] + b_ada[l]).reshape(B, N_MOD, D_MODEL)
        h = modulate(rms_norm_2(x, norm_gain[l, 0]), mod[:, 0], mod[:, 1])
        x = x + 0.5 * mod[:, 2][:, None, :] * swiglu(h, ffn_w_gate[l, 0], ffn_w_up[l, 0], ffn_w_down[l, 0])
        h = modulate(rms_norm_2(x, norm_gain[l, 1]), mod[:, 3], mod[:, 4])
        x = x + mod[:, 5][:, None, :] * hybrid_mixer(h, w_in[l], qk_gain[l], rel_bias[l], forget_bias[l],
                                                      w_pool[l], pool_scale[l], w_branch[l], w_out[l])
        h = modulate(rms_norm_2(x, norm_gain[l, 2]), mod[:, 6], mod[:, 7])
        x = x + 0.5 * mod[:, 8][:, None, :] * swiglu(h, ffn_w_gate[l, 1], ffn_w_up[l, 1], ffn_w_down[l, 1])
    return x


def setup_inputs(seed=0):
    out = dict(first_inputs(seed))
    for name, value in second_inputs(seed + 1).items():
        if name != "x":
            out[name + "_2"] = value
    return out


def reference(
    x, w_in, qk_gain, diff_lambda, diff_subln, sinks, cmp_pos, cmp_w1, cmp_w2, w_branch, w_out,
    norm_mix, norm_mlp, w_up, w_down, rel_bias, c_2, w_ada_2, b_ada_2, norm_gain_2,
    ffn_w_gate_2, ffn_w_up_2, ffn_w_down_2, w_in_2, qk_gain_2, rel_bias_2, forget_bias_2,
    w_pool_2, pool_scale_2, w_branch_2, w_out_2,
):
    x = first_block(
        x, w_in, qk_gain, diff_lambda, diff_subln, sinks, cmp_pos, cmp_w1, cmp_w2, w_branch,
        w_out, norm_mix, norm_mlp, w_up, w_down, rel_bias,
    )
    return second_block(
        x, c_2, w_ada_2, b_ada_2, norm_gain_2, ffn_w_gate_2, ffn_w_up_2, ffn_w_down_2, w_in_2,
        qk_gain_2, rel_bias_2, forget_bias_2, w_pool_2, pool_scale_2, w_branch_2, w_out_2,
    )


_drawn_inputs = setup_inputs


def setup_inputs(seed=0):
    import zlib

    import numpy as np

    out = dict(_drawn_inputs(seed))
    spreads = {}
    factors = {'diff_lambda': 8.0,
     'sinks': 8.0,
     'b_ada_2': 3.755,
     'norm_gain_2': 4.495,
     'qk_gain_2': 8.0,
     'rel_bias_2': 8.0,
     'pool_scale_2': 8.0}
    for name, (base, spread) in spreads.items():
        noise = np.random.default_rng([zlib.crc32(name.encode()), seed]).standard_normal(out[name].shape)
        drawn = base * np.exp(spread * noise) if base else spread * noise
        out[name] = __import__('jax').numpy.asarray(drawn.astype(out[name].dtype))
    for name, factor in factors.items():
        out[name] = (out[name] * factor).astype(out[name].dtype)
    return out
```

```python
import numpy as np
import concourse.bass as bass
from concourse import mybir
from contextlib import ExitStack, contextmanager

F32 = mybir.dt.float32
F32R = mybir.dt.float32r
ACT = mybir.ActivationFunctionType
ALU = mybir.AluOpType

P = 128
S = 512
D = 1024
KC = D // P
TB = S // P
EPS = 1e-6
PIECES = 4
HALF = 64
CMP_N = 31
CMP_STRIDE = 16
NEG = -1e30
LAM_INIT = 0.2
V_BC = 408
SLOT = 9 * P
RAW = PIECES * SLOT
MODS = 72
GATES = 24
ADA = 3
FFN_PARTS = (8, 8, 6)
UNITS = dict(att_a=8, att_b=8, att_c=24, att_a2=8, att_c2=8)
TILES = dict(att_a=1, att_b=2, att_c=2, att_a2=2, att_c2=2)
SM = dict(mix=0, mlp=8, gain=16, subln=24, sinks=25, pos=33, w2=65)
SM_N = 65 + 2 * 2 * HALF
LY = dict(gain=0, b_ada=24, pool=96, pool_scale=608, qk=612, f_bias=616)
LY_N = 617
CS = dict(ident=0, pair_ones=128, tri=256, window=384, chunk=512, cmask=640, valid=764, inv_count=765)
CS_N = 765 + 64


class Phase:

    def __init__(self, name, kind, groups=(), **totals):
        self.name, self.kind, self.groups, self.totals = name, kind, list(groups), dict(totals)
        n = sum(g for g, _ in self.groups)
        self.totals.update(w_hi=PIECES * n, w_lo=PIECES * n, w_used=PIECES * n, group=n, phase_done=3)
        self.floats = sum(g * PIECES * f * P for g, f in self.groups)


def norm_phase(name):
    return Phase(name, "norm", norm_squared=KC, norm_summed=KC, norm_inverse=1, norm_rstd=1,
                 norm_scaled=KC, h_hi=KC)


def attention_phase(kind):
    n = 4 * UNITS[kind]
    return Phase(kind, kind, scores=n, row_max=n, exps=n, probs=n, transposed=n, pt_copied=n,
                 pv=n, pair_done=4, staged=4, bias0=32 * TILES[kind], bias1=32 * TILES[kind])


def proj_phase(name, groups, normed, plain):
    return Phase(name, name, groups, qk_squared=normed, qk_summed=normed, qk_inverse=normed,
                 qk_rstd=normed, qk_out=normed, plain_out=plain)


def up_phase(name, kind, groups, blocks):
    return Phase(name, kind, [(groups, KC * P)], gated=blocks, product=blocks, act_hi=blocks, act_lo=blocks)


def down_phase(name, tiles):
    return Phase(name, "down", [(2, tiles * P)], x_added=KC)


def mix_phases(tag):
    return [
        Phase("split" + tag, "split" + tag, br_hi=12,
              **(dict(qk_squared=4, qk_summed=4, qk_inverse=4, qk_rstd=4, qk_out=4) if tag == "1" else {})),
        Phase("merge" + tag, "merge", [(KC, SLOT)], gate_sig=3 * KC, y_read=3 * KC),
        Phase("msplit" + tag, "msplit", h_hi=KC),
        down_phase("wout" + tag, KC),
    ]


def ffn_phases(tag):
    out = [norm_phase("norm" + tag)]
    for n, chunks in enumerate(FFN_PARTS):
        out += [up_phase(f"up{tag}{n}", "ffn_up", chunks // 2, chunks), down_phase(f"down{tag}{n}", chunks)]
    return out


FULL = KC * P
FIRST = ([Phase("prep", "prep", pair_done=2, prep_loaded=96, prep_step=5), norm_phase("norm_mix"),
          proj_phase("proj_a", [(3, FULL)], 8, 4), attention_phase("att_a"),
          proj_phase("proj_bc", [(2, FULL), (1, 2 * P), (1, 2 * V_BC)], 7, 6), attention_phase("att_b"),
          proj_phase("proj_cq", [(1, FULL)], 4, 0),
          Phase("compress", "compress", cmp_loaded=32, cmp_pe=5, cmp_dve=4, cmp_act=5), attention_phase("att_c")]
         + mix_phases("1") + [norm_phase("norm_mlp")])
MLP = [up_phase("mlp_up", "mlp_up", 2, 8), down_phase("mlp_down", KC)]
MLP[0].totals.update(ada0=16 * 3, ada1=16 * 3, ada_used=6)
MLP[1].totals.update(ada0=16 * 3, ada1=16 * 3, ada_used=6)
LAYER = ([Phase("layer", "layer", layer_loaded=16)] + ffn_phases("a")
         + [norm_phase("norm_l"),
            proj_phase("proj_a2", [(3, FULL)], 8, 4), attention_phase("att_a2"),
            proj_phase("proj_u", [(1, FULL), (1, 2 * P)], 0, 5),
            Phase("pool", "pool", pool_in=4, pool_mm=4, pool_out=4, forget_step=2, forget_dve=3, cum_stored=16),
            proj_phase("proj_c2", [(3, FULL)], 8, 4), attention_phase("att_c2")]
         + mix_phases("2") + ffn_phases("b"))
SEGMENTS = [("first", FIRST, 1), ("mlp", MLP, 4), ("layer", LAYER, 2)]
PRESET = dict(w_lo=2 * PIECES, w_used=PIECES, ada_used=2)


def starts():
    at, per, now = {}, {}, dict(PRESET)
    for seg, phases, turns in SEGMENTS:
        entry = dict(now)
        for ph in phases:
            at[ph.name] = dict(now)
            for name, n in ph.totals.items():
                now[name] = now.get(name, 0) + n
        per[seg] = {name: n - entry.get(name, 0) for name, n in now.items()}
        assert turns == 1 or per[seg]["group"] % 2 == 0
        for name, n in per[seg].items():
            now[name] += n * (turns - 1)
    return at, per


START, PER = starts()
SEMS = sorted({s for _, phases, _ in SEGMENTS for ph in phases for s in ph.totals} - {"group"})

CHAIN = {'pool0': 4, 'pool6': 4, 'pool7': 4, 'act5': 1, 'dve0': 40, 'dve1': 48, 'dve2': 148, 'dve3': 4, 'dve4': 28, 'dve6': 32, 'dve7': 32, 'dve8': 4, 'dve5': 240, 'pool5': 16}
WANTED = {}


class Engine:

    def __init__(self, eng, name):
        self.e, self.name = eng, name
        self.phase = None
        self.seg, self.turn = "first", None
        self.base, self.n, self.loops = 0, 0, 0

    def at(self, sem, more):
        v = START[self.phase].get(sem, 0)
        per = PER[self.seg].get(sem, 0)
        if self.turn is not None and per:
            return self.turn * per + (more + v)
        return more + v

    def step(self):
        self.n += 1
        return self.base + self.n

    @contextmanager
    def loop(self, turns):
        key = f"{self.name}{self.loops}"
        self.loops += 1
        per = CHAIN.get(key, 0)
        base, n = self.base, self.n
        self.e.nop(nofuse=True)
        with self.e.Fori(0, turns) as it:
            if per:
                self.base = it * per + base
            yield it
        if self.n - n != per:
            WANTED[key] = self.n - n
        self.base, self.n = base, n + turns * per

    @contextmanager
    def segment(self, name, turns):
        with self.loop(turns) as it:
            self.seg, self.turn = name, it
            yield it
        self.seg, self.turn = "first", None


def walk(E, run):
    def phases(part):
        for ph in part:
            E.phase = ph.name
            run(ph)

    phases(FIRST)
    with E.segment("mlp", 4):
        phases(MLP)
    with E.segment("layer", 2):
        phases(LAYER)


def group_loop(E, count, parity):
    yield 0, parity, True
    turns = (count - 1) // 2
    if turns >= 2:
        with E.loop(turns) as it:
            for u in (0, 1):
                yield it * 2 + (1 + u), (parity + 1 + u) % 2, False
    else:
        for g in range(1, 1 + 2 * turns):
            yield g, (parity + g) % 2, False
    if (count - 1) % 2:
        yield count - 1, (parity + count - 1) % 2, False


def groups_of(E, ph):
    done = 0
    for r, (count, _) in enumerate(ph.groups):
        for g, par, first in group_loop(E, count, (START[ph.name].get("group", 0) + done) % 2):
            yield g + done, g, r, par, first and done == 0
        done += count


def row(t, i):
    return t[:, bass.ds(i, 1), :].rearrange("p a s -> p (a s)")


def units_of(kind):
    out = []
    for i in range(TB):
        for half in (0, 1):
            if kind == "att_c":
                out += [(half, i, b, 0, i + 1) for b in ("win", "sel")] + [(half, i, "cmp", 0, 1)]
            elif kind == "att_b":
                lo = max(0, i - 1)
                out.append((half, i, "one", lo, i + 1 - lo))
            else:
                out.append((half, i, "one", 0, i + 1))
    return out


def build(nc, x_in, w_first, w_mlp, w_layer, ada, first_small, layer_small, biases, cmp_w1, lam_in, c_in,
          consts, out):
    ctx = ExitStack()
    with ctx:
        def sb(name, shape, dt=F32):
            return ctx.enter_context(nc.sbuf_tensor(name, shape, dt))

        x = sb("x", [P, KC, S])
        h_hi = sb("h_hi", [P, KC, S], F32R)
        h_lo = sb("h_lo", [P, KC, S], F32R)
        raw = sb("raw", [P, 2, RAW])
        w_hi = sb("w_hi", [P, PIECES, SLOT], F32R)
        w_lo = sb("w_lo", [P, PIECES, SLOT], F32R)
        small = sb("small", [P, SM_N])
        lay = sb("lay", [P, LY_N])
        cst = sb("cst", [P, CS_N])
        ones = sb("ones", [P, P])
        mods = sb("mods", [P, 2 * MODS])
        mod = sb("mod", [P, MODS])
        mod_part = sb("mod_part", [P, 3 * ADA])
        norm_a = sb("norm_a", [P, KC])
        norm_b = sb("norm_b", [P, KC])
        res_scale = sb("res_scale", [P, KC])
        gates = sb("gates", [P, TB, GATES])
        kc_sb = sb("kc_sb", [P, CMP_N])
        vc_sb = sb("vc_sb", [CMP_N, P])
        row_max = sb("row_max", [P, 2])
        neg_max = sb("neg_max", [P, 2])
        row_sum = sb("row_sum", [P, 2])
        row_inv = sb("row_inv", [P, 2])
        row_scale = sb("row_scale", [P, 2])
        neg_lam = sb("neg_lam", [P, 1])
        lam_t = sb("lam_t", [P, 4])
        tiny_t = sb("tiny_t", [P, 1])

        arena_kb = 78.125
        arena = sb("arena", [P, int(arena_kb * 256)])
        first_byte = nc.sbuf_base - int(arena_kb * 1024)

        def at(name, kb, shape, dt=F32):
            assert kb * 1024 + int(np.prod(shape[1:])) * 4 <= arena_kb * 1024, name
            return nc.alloc_sbuf_tensor_at(name, shape, dt, offset=first_byte + int(kb * 1024))

        qk = at("qk", 0, [P, 9, S])
        v_all = at("v_all", 18, [P, TB, S])
        v_bc = at("v_bc", 18, [P, TB, V_BC])
        branch = at("branch", 26, [P, 3 * 4, S])
        q_st = at("q_st", 50, [P, 2, S])
        k_st = at("k_st", 54, [P, 2, S])
        v_st = at("v_st", 58, [P, 2, TB, P])
        s_sb = at("s_sb", 62, [P, 2, S + 8])
        pt_sb = at("pt_sb", 66.0625, [P, 2, S])
        bias_t = at("bias_t", 70.0625, [P, 2, 2, S])
        c_t = at("c_t", 50, [P, D])
        lam_w = at("lam_w", 54, [P, 4, HALF])
        sq_t = at("sq_t", 50, [P, 2, S])
        inv_t = at("inv_t", 54, [P, 2, S])
        rs_t = at("rs_t", 58, [P, 2, S])
        cmp_w = at("cmp_w", 50, [P, CMP_STRIDE, 2 * P])
        cmp_t = at("cmp_t", 66, [P, 2, S])
        cmp_x = at("cmp_x", 70, [P, CMP_STRIDE, 2, CMP_N])
        cmp_h = at("cmp_h", 74, [P, 2, 2 * CMP_N])
        cmp_s = at("cmp_s", 75, [P, 2, CMP_N])
        pool_s = at("pool_s", 50, [P, 2, S])
        pool_d = at("pool_d", 54, [P, S])
        f_t = at("f_t", 56, [8, 5, S])
        br_hi = at("br_hi", 0, [P, 12, S], F32R)
        br_lo = at("br_lo", 50, [P, 12, S], F32R)
        merged = at("merged", 26, [P, KC, S])
        sig_t = at("sig_t", 42, [P, 3, S])
        prod_t = at("prod_t", 48, [P, S])
        nsq = at("nsq", 60, [P, 2, S])
        ninv = at("ninv", 64, [P, S])
        nrs = at("nrs", 66, [P, S])
        nt = at("nt", 68, [P, 2, S])
        a_hi = at("a_hi", 0, [P, KC, S], F32R)
        a_lo = at("a_lo", 16, [P, KC, S], F32R)
        g_sb = at("g_sb", 32, [P, 2, S])
        ada_t = at("ada_t", 36, [P, 2, ADA, D])

        psum = ctx.enter_context(nc.psum_tensor("psum", [P, 8 * S], F32))

        def bank(b, n=S):
            return psum[:, b * S:b * S + n]

        c_bcast = psum[:, 6 * S:8 * S]
        ada_junk = psum[:, 4 * S:6 * S]
        cum_dram = nc.dram_tensor("cum_dram", (8, S), F32).ap()

        sem = {n: ctx.enter_context(nc.semaphore(n)) for n in SEMS}
        raw_loaded, bias_loaded, ada_loaded = [ctx.enter_context(nc.semaphore(f"raw_loaded{i}")) for i in (0, 1)], \
            (sem["bias0"], sem["bias1"]), (sem["ada0"], sem["ada1"])
        act_chain, dve_chain, pool_chain = (ctx.enter_context(nc.semaphore(f"{n}_chain"))
                                            for n in ("act", "dve", "pool"))
        out_done = ctx.enter_context(nc.semaphore("out_done"))
        ident = cst[:, CS["ident"]:CS["ident"] + P]
        pair_ones = cst[:, CS["pair_ones"]:CS["pair_ones"] + P]
        block = ctx.enter_context(nc.Block())

        @block.sync
        def _(sp):
            E = Engine(sp, "sp")
            offset = {"first": 0, "mlp": 0, "layer": 0}

            sp.dma_start(small[:], first_small).then_inc(sem["prep_loaded"], 16)
            sp.dma_start(cst[:], consts).then_inc(sem["prep_loaded"], 16)
            sp.dma_start(c_t[:], c_in).then_inc(sem["prep_loaded"], 16)
            sp.dma_start(lam_w[:], lam_in).then_inc(sem["prep_loaded"], 16)
            sp.dma_start(x[:, 0:4, :], x_in[:, 0:4, :]).then_inc(sem["prep_loaded"], 16)
            sp.dma_start(x[:, 4:8, :], x_in[:, 4:8, :]).then_inc(sem["prep_loaded"], 16)

            def run(ph):
                src = {"first": w_first, "mlp": w_mlp, "layer": w_layer}[E.seg]
                for gi, g, r, par, first in groups_of(E, ph):
                    size = ph.groups[r][1]
                    n = PIECES * size
                    at_run = offset[E.seg] + sum(c * PIECES * f * P for c, f in ph.groups[:r])
                    start = g * (n * P) + at_run
                    if E.turn is not None:
                        start = E.turn * sum(q.floats for q in dict(mlp=MLP, layer=LAYER)[E.seg]) + start
                    sp.wait_ge(sem["w_lo"], E.at("w_lo", gi * PIECES - PIECES))
                    sp.dma_start(raw[:, par, 0:n],
                                 src[bass.ds(start, n * P)].rearrange("(p n) -> p n", p=P))\
                        .then_inc(raw_loaded[par], 16)
                offset[E.seg] += ph.floats

            walk(E, run)
            sp.wait_ge(sem["phase_done"], sum(ph.totals["phase_done"] * n for _, phases, n in SEGMENTS for ph in phases))
            sp.dma_start(out, x[:]).then_inc(out_done, 16)
            sp.wait_ge(out_done, 16)

        @block.gpsimd
        def _(pool):
            E = Engine(pool, "pool")
            nc.gpsimd.memset(ones[:], 1.0).then_inc(pool_chain, 1)
            pool.wait_ge(pool_chain, E.step())
            pool.nop().then_inc(sem["prep_step"], 1)
            pool.nop().then_inc(sem["w_lo"], PRESET["w_lo"])
            pool.nop().then_inc(sem["pair_done"], 2)

            def raw_count(ph, gi, par):
                before = gi + START[ph.name].get("group", 0)
                if E.turn is not None:
                    before = E.turn * PER[E.seg]["group"] + before
                return before

            def split(ph):
                for gi, g, r, par, first in groups_of(E, ph):
                    size = ph.groups[r][1]
                    pool.wait_ge(raw_loaded[par], raw_count(ph, gi, par) * 8 + (16 if par == 0 else 8))
                    for k in range(PIECES):
                        piece = raw[:, par, k * size:(k + 1) * size]
                        pool.wait_ge(sem["w_used"], E.at("w_used", gi * PIECES + k + 1 - PIECES))
                        nc.gpsimd.tensor_tensor(w_hi[:, k, 0:size], piece, ones[:, 0:1].to_broadcast([P, size]),
                                                ALU.mult)\
                            .then_inc(sem["w_hi"], 1)
                        pool.wait_ge(sem["w_hi"], E.at("w_hi", gi * PIECES + k + 1))
                        nc.gpsimd.tensor_tensor(w_lo[:, k, 0:size], piece, w_hi[:, k, 0:size].bitcast(F32),
                                                ALU.subtract).then_inc(sem["w_lo"], 1)

            def stage(ph):
                kind = ph.kind
                pool.wait_ge(sem["phase_done"], E.at("phase_done", 0))
                pool.nop(nofuse=True)
                tile0 = dict(att_a=0, att_b=4, att_c=12, att_a2=20, att_c2=0)[kind]
                with E.loop(2) as it:
                    for u in (0, 1):
                        pair = it * 2 + u
                        pool.wait_ge(sem["pair_done"], E.at("pair_done", it * 2 + u - 1))
                        pool.nop(nofuse=True)
                        for t in range(TILES[kind]):
                            if kind == "att_c2":
                                src = cum_dram[bass.ds(pair * 2 + t, 1), :].to_broadcast([P, S])
                            else:
                                tile = pair * TILES[kind] + (t + tile0)
                                if kind == "att_a2":
                                    tile = E.turn * 8 + tile
                                src = biases[bass.ds(tile, 1), :, :].rearrange("a p s -> p (a s)")
                            pool.dma_start(bias_t[:, u, t, :], src).then_inc(bias_loaded[u], 16)
                        if kind in ("att_a", "att_a2", "att_c2"):
                            nc.gpsimd.tensor_copy(k_st[:, u, :], row(qk, it * 2 + (4 + u))).then_inc(pool_chain, 1)
                            pool.wait_ge(pool_chain, E.step())
                            nc.gpsimd.tensor_copy(v_st[:, u, :, :],
                                                  v_all[:, :, bass.ds(it * (2 * P) + u * P, P)]).then_inc(pool_chain, 1)
                            pool.wait_ge(pool_chain, E.step())
                        nc.gpsimd.tensor_copy(q_st[:, u, :], row(qk, pair))\
                            .then_inc(sem["staged"], 1)

            def run(ph):
                if ph.groups:
                    split(ph)
                if ph.kind.startswith("att"):
                    stage(ph)

            walk(E, run)

        @block.tensor
        def _(pe):
            E = Engine(pe, "pe")
            mm = nc.tensor.matmul
            pe.nop().then_inc(sem["w_used"], PRESET["w_used"])

            def mm3(dst, lh, ll, rh, rl, first, last):
                mm(dst, lh, rh, start=first, stop=False)
                mm(dst, lh, rl, start=False, stop=False)
                return mm(dst, ll, rh, start=False, stop=last)

            def piece_ready(ph, gi, k):
                pe.wait_ge(sem["w_lo"], E.at("w_lo", gi * PIECES + k + 1))

            def tiles(dst, k, t0, n, hi, lo, c0, first, last):
                for t in range(n):
                    w = slice((t0 + t) * P, (t0 + t + 1) * P)
                    ins = mm3(dst, w_hi[:, k, w], w_lo[:, k, w], hi[:, c0 + t, :], lo[:, c0 + t, :],
                              first and t == 0, last and t == n - 1)
                return ins

            def norm(ph):
                for c in range(KC):
                    pe.wait_ge(sem["norm_squared"], E.at("norm_squared", c + 1))
                    mm(bank(4), ones[:], nsq[:, c % 2, :], start=c == 0, stop=c == KC - 1)\
                        .then_inc(sem["norm_summed"], 1)

            def qk_sum(ph, j, n):
                pe.wait_ge(sem["qk_squared"], E.at("qk_squared", j + 1))
                if j >= 2:
                    pe.wait_ge(sem["qk_inverse"], E.at("qk_inverse", j - 1))
                mm(bank(4 + j % 2, n), pair_ones, sq_t[:, j % 2, 0:n], start=True, stop=True)\
                    .then_inc(sem["qk_summed"], 1)

            def full_group(ph, gi, free):
                for k in range(PIECES):
                    piece_ready(ph, gi, k)
                    if free:
                        free(k)
                    tiles(bank(k), k, 0, KC, h_hi, h_lo, 0, True, True).then_inc(sem["w_used"], 1)
                    yield k

            def thin_group(ph, gi, b, free):
                for k in range(PIECES):
                    piece_ready(ph, gi, k)
                    if k == 0 and free:
                        free()
                    tiles(bank(b), k, 0, 2, h_hi, h_lo, 2 * k, k == 0, k == PIECES - 1)\
                        .then_inc(sem["w_used"], 1)

            def token_group(ph, gi, cols, free):
                for k in range(PIECES):
                    piece_ready(ph, gi, k)
                    for t in range(2):
                        c = 2 * k + t
                        w = slice(t * cols, (t + 1) * cols)
                        for b in range(TB):
                            if c == 0 and free:
                                free(b)
                            tok = slice(b * P, (b + 1) * P)
                            ins = mm3(bank(b, cols), h_hi[:, c, tok], h_lo[:, c, tok], w_hi[:, k, w],
                                      w_lo[:, k, w], c == 0, c == KC - 1)
                    ins.then_inc(sem["w_used"], 1)

            def proj(ph):
                kind = ph.kind
                if kind in ("proj_a", "proj_a2", "proj_c2"):
                    for g in range(2):
                        free = (lambda k: pe.wait_ge(sem["qk_out"], E.at("qk_out", k + 1))) if g else None
                        for k in full_group(ph, g, free):
                            if k:
                                qk_sum(ph, 4 * g + k - 1, S)
                        qk_sum(ph, 4 * g + 3, S)
                    token_group(ph, 2, S, lambda b: pe.wait_ge(sem["qk_out"], E.at("qk_out", 4 + b + 1)))
                elif kind == "proj_bc":
                    for k in full_group(ph, 0, None):
                        if k:
                            qk_sum(ph, k - 1, S)
                    qk_sum(ph, 3, S)
                    for k in full_group(ph, 1, lambda k: pe.wait_ge(sem["qk_out"], E.at("qk_out", k + 1))):
                        if k:
                            qk_sum(ph, 4 + k - 1, S)
                    thin_group(ph, 2, 0, lambda: pe.wait_ge(sem["qk_out"], E.at("qk_out", 5)))
                    def free(b):
                        if b == 0:
                            pe.wait_ge(sem["plain_out"], E.at("plain_out", 2))
                        elif b == 3:
                            pe.wait_ge(sem["plain_out"], E.at("plain_out", 1))
                        else:
                            pe.wait_ge(sem["qk_out"], E.at("qk_out", 5 + b))
                    token_group(ph, 3, V_BC, free)
                elif kind == "proj_cq":
                    for k in full_group(ph, 0, None):
                        if k:
                            qk_sum(ph, k - 1, S)
                    qk_sum(ph, 3, S)
                elif kind == "proj_u":
                    for k in full_group(ph, 0, None):
                        pass
                    thin_group(ph, 1, 4, None)

            def attention(ph):
                kind = ph.kind
                units = units_of(kind)
                n = len(units)
                masks = {"tri": CS["tri"], "window": CS["window"], "chunk": CS["chunk"]}
                with E.loop(2) as it:
                    def score(j):
                        u, (half, i, br, lo, blocks) = j // n, units[j % n]
                        rows = slice(half * HALF, (half + 1) * HALF)
                        if j % n == 0:
                            pe.wait_ge(sem["staged"], E.at("staged", it * 2 + u + 1))
                        q = q_st[rows, u, i * P:(i + 1) * P]
                        b = bank(j % 2)
                        pe.nop(nofuse=True)
                        if br == "cmp":
                            mm(b[:, 0:CMP_N], q, kc_sb[rows, :], start=True, stop=True)\
                                .then_inc(sem["scores"], 1)
                            return
                        cols = slice(lo * P, (lo + blocks) * P)
                        k = {"att_b": qk[rows, 4, cols], "att_c": qk[rows, 5 if br == "sel" else 6, cols]}\
                            .get(kind, k_st[rows, u, cols])
                        w = blocks * P
                        mm(b[:, 0:w], q, k, start=True, stop=False)
                        tri = masks["chunk" if kind == "att_a2" else "tri"]
                        if kind == "att_b" and blocks == 2:
                            mm(b[:, 0:P], ident, cst[:, masks["window"]:masks["window"] + P],
                               start=False, stop=False)
                        mm(b[:, w - P:w], ident, cst[:, tri:tri + P], start=False, stop=True)\
                            .then_inc(sem["scores"], 1)

                    score(0)
                    for j in range(2 * n):
                        if j + 1 < 2 * n:
                            score(j + 1)
                        u, (half, i, br, lo, blocks) = j // n, units[j % n]
                        pe.wait_ge(sem["probs"], E.at("probs", it * (2 * n) + j + 1))
                        t_bank = bank(2 + j % 2)
                        pe.nop(nofuse=True)
                        if br == "cmp":
                            nc.tensor.transpose(t_bank[0:CMP_N, 0:P], s_sb[:, j % 2, 0:CMP_N], ident)\
                                .then_inc(sem["transposed"], 1)
                        else:
                            for b in range(blocks):
                                ins = nc.tensor.transpose(t_bank[:, b * P:(b + 1) * P],
                                                          s_sb[:, j % 2, b * P:(b + 1) * P], ident)
                            ins.then_inc(sem["transposed"], 1)
                        pe.wait_ge(sem["pt_copied"], E.at("pt_copied", it * (2 * n) + j + 1))
                        pe.nop(nofuse=True)
                        wide = kind == "att_a"
                        o = psum[slice(0, P) if wide else slice(half * HALF, (half + 1) * HALF),
                                 (4 + u) * S + i * P:(4 + u) * S + (i + 1) * P]
                        start = {"att_a": half == 0, "att_c": br == "win"}.get(kind, True)
                        stop = {"att_a": half == 1, "att_c": br == "cmp"}.get(kind, True)
                        if br == "cmp":
                            ins = mm(o, vc_sb[:, half * HALF:(half + 1) * HALF], pt_sb[0:CMP_N, j % 2, 0:P],
                                     start=False, stop=True)
                        else:
                            for b in range(blocks):
                                if kind == "att_b":
                                    v = v_bc[:, lo + b, half * HALF:(half + 1) * HALF]
                                elif kind == "att_c":
                                    c = (P if br == "sel" else 2 * P) + half * HALF
                                    v = v_bc[:, lo + b, c:c + HALF]
                                elif wide:
                                    v = v_st[:, u, b, :]
                                else:
                                    v = v_st[:, u, b, half * HALF:(half + 1) * HALF]
                                ins = mm(o, v, pt_sb[:, j % 2, b * P:(b + 1) * P],
                                         start=start and b == 0, stop=stop and b == blocks - 1)
                        ins.then_inc(sem["pv"], 1)

            def compress(ph):
                for kv in (0, 1):
                    pe.wait_ge(sem["cmp_loaded"], E.at("cmp_loaded", 16 * (kv + 1)))
                    pe.wait_ge(sem["cmp_dve"], E.at("cmp_dve", 3 * kv + 1))
                    for hid in (0, 1):
                        for j in range(CMP_STRIDE):
                            ins = mm(bank(hid, 2 * CMP_N), cmp_w[:, j, hid * P:(hid + 1) * P],
                                     cmp_x[:, j, :, :].rearrange("p g c -> p (g c)"),
                                     start=j == 0, stop=j == CMP_STRIDE - 1)
                    ins.then_inc(sem["cmp_pe"], 1)
                    pe.wait_ge(sem["cmp_act"], E.at("cmp_act", 3 * kv + 1))
                    pe.nop(nofuse=True)
                    for g in (0, 1):
                        for hid in (0, 1):
                            w2 = small[:, SM["w2"] + (2 * kv + hid) * HALF:SM["w2"] + (2 * kv + hid + 1) * HALF]
                            hx = cmp_h[:, hid, g * CMP_N:(g + 1) * CMP_N]
                            if kv == 0:
                                ins = mm(psum[g * HALF:(g + 1) * HALF, 2 * S:2 * S + CMP_N], w2, hx,
                                         start=hid == 0, stop=hid == 1)
                            else:
                                ins = mm(psum[0:CMP_N, 2 * S + g * HALF:2 * S + (g + 1) * HALF], hx, w2,
                                         start=hid == 0, stop=hid == 1)
                    ins.then_inc(sem["cmp_pe"], 1)
                    if kv == 0:
                        pe.wait_ge(sem["cmp_act"], E.at("cmp_act", 2))
                        mm(bank(3, CMP_N), pair_ones, cmp_s[:, 0, :], start=True, stop=True)\
                            .then_inc(sem["cmp_pe"], 1)

            def merge(ph):
                for gi, g, r, par, first in groups_of(E, ph):
                    for k in range(PIECES):
                        piece_ready(ph, gi, k)
                        for t in range(k * 9, (k + 1) * 9):
                            n, s_ = t // 12, t % 12
                            gate = s_ < KC
                            if not first and s_ == 0:
                                pe.wait_ge(sem["gate_sig"], E.at("gate_sig", g * 3 + n - 2))
                            if not first and s_ == KC:
                                pe.wait_ge(sem["y_read"], E.at("y_read", g * 3 + n - 2))
                            w = slice((t % 9) * P, (t % 9 + 1) * P)
                            c = s_ if gate else 4 * n + s_ - KC
                            hi, lo = (h_hi, h_lo) if gate else (br_hi, br_lo)
                            ins = mm3(bank(2 * n + (not gate)), w_hi[:, k, w], w_lo[:, k, w], hi[:, c, :],
                                      lo[:, c, :], s_ in (0, KC), s_ in (KC - 1, 11))
                        ins.then_inc(sem["w_used"], 1)

            def split_a(ph):
                for j in range(4):
                    pe.wait_ge(sem["qk_squared"], E.at("qk_squared", j + 1))
                    if j >= 2:
                        pe.wait_ge(sem["qk_inverse"], E.at("qk_inverse", j - 1))
                    mm(bank(4 + j % 2), ones[:], sq_t[:, j % 2, :], start=True, stop=True)\
                        .then_inc(sem["qk_summed"], 1)

            def up(ph):
                ffn = ph.kind == "ffn_up"
                for gi, g, r, par, first in groups_of(E, ph):
                    for k in range(PIECES):
                        piece_ready(ph, gi, k)
                        if not first:
                            if ffn and k % 2:
                                pe.wait_ge(sem["product"], E.at("product", g * 2 + (k // 2 - 1)))
                            elif ffn:
                                pe.wait_ge(sem["gated"], E.at("gated", g * 2 + (k // 2 - 1)))
                            else:
                                pe.wait_ge(sem["product"], E.at("product", g * 4 + (k - 3)))
                        tiles(bank(k), k, 0, KC, h_hi, h_lo, 0, True, True).then_inc(sem["w_used"], 1)

            def down(ph):
                n = ph.groups[0][1] // P
                hi, lo = (h_hi, h_lo) if ph.name.startswith("wout") else (a_hi, a_lo)
                for gi, g, r, par, first in groups_of(E, ph):
                    for k in range(PIECES):
                        piece_ready(ph, gi, k)
                        if not first:
                            pe.wait_ge(sem["x_added"], E.at("x_added", g * 4 + (k - 3)))
                        tiles(bank(k), k, 0, n, hi, lo, 0, True, True).then_inc(sem["w_used"], 1)

            def pool_mix(ph):
                for g in range(4):
                    pe.wait_ge(sem["pool_in"], E.at("pool_in", g + 1))
                    if g >= 2:
                        pe.wait_ge(sem["pool_out"], E.at("pool_out", g - 1))
                    w = lay[:, LY["pool"] + g * P:LY["pool"] + (g + 1) * P]
                    mm(bank(g % 2), w, pool_d[:], start=True, stop=True).then_inc(sem["pool_mm"], 1)

            def run(ph):
                kind = ph.kind
                if kind == "prep":
                    pe.wait_ge(sem["prep_step"], E.at("prep_step", 5))
                elif kind == "norm":
                    norm(ph)
                elif kind.startswith("proj"):
                    proj(ph)
                elif kind.startswith("att"):
                    attention(ph)
                elif kind == "compress":
                    compress(ph)
                elif kind == "split1":
                    split_a(ph)
                elif kind == "merge":
                    merge(ph)
                elif kind.endswith("up"):
                    up(ph)
                elif kind == "down":
                    down(ph)
                elif kind == "pool":
                    pool_mix(ph)
                pe.nop(nofuse=True)
                pe.drain().then_inc(sem["phase_done"], 1)
                pe.wait_ge(sem["phase_done"], E.at("phase_done", 3))

            walk(E, run)

        @block.scalar
        def _(act):
            E = Engine(act, "act")
            fn = nc.scalar.activation

            def norm(ph):
                for c in range(KC):
                    if c >= 2:
                        act.wait_ge(sem["norm_summed"], E.at("norm_summed", c - 1))
                    fn(nsq[:, c % 2, :], x[:, c, :], ACT.Square).then_inc(sem["norm_squared"], 1)
                act.wait_ge(sem["norm_inverse"], E.at("norm_inverse", 1))
                fn(nrs[:], ninv[:], ACT.Sqrt).then_inc(sem["norm_rstd"], 1)
                for c in range(KC):
                    act.wait_ge(sem["norm_scaled"], E.at("norm_scaled", c + 1))
                    fn(h_hi[:, c, :], nt[:, c % 2, :], ACT.Identity, bias=norm_b[:, c:c + 1])\
                        .then_inc(sem["h_hi"], 1)

            def square(ph, j, src, n=S):
                if j >= 2:
                    act.wait_ge(sem["qk_summed"], E.at("qk_summed", j - 1))
                fn(sq_t[:, j % 2, 0:n], src, ACT.Square).then_inc(sem["qk_squared"], 1)

            def root(ph, j, n=S):
                act.wait_ge(sem["qk_inverse"], E.at("qk_inverse", j + 1))
                if j >= 2:
                    act.wait_ge(sem["qk_out"], E.at("qk_out", j - 1))
                fn(rs_t[:, j % 2, 0:n], inv_t[:, j % 2, 0:n], ACT.Sqrt).then_inc(sem["qk_rstd"], 1)

            def normed_blocks(ph, gi, j0, n):
                for k in range(n):
                    act.wait_ge(sem["w_used"], E.at("w_used", gi * PIECES + k + 1))
                    square(ph, j0 + k, bank(k))
                    if k:
                        root(ph, j0 + k - 1)
                root(ph, j0 + n - 1)

            def proj(ph):
                kind = ph.kind
                if kind in ("proj_a", "proj_a2", "proj_c2"):
                    normed_blocks(ph, 0, 0, 4)
                    normed_blocks(ph, 1, 4, 4)
                    act.wait_ge(sem["w_used"], E.at("w_used", 12))
                    for b in range(TB):
                        fn(v_all[:, b, :], bank(b), ACT.Copy).then_inc(sem["plain_out"], 1)
                elif kind == "proj_bc":
                    normed_blocks(ph, 0, 0, 4)
                    normed_blocks(ph, 1, 4, 3)
                    act.wait_ge(sem["w_used"], E.at("w_used", 8))
                    fn(qk[:, 7, :], bank(3), ACT.Copy).then_inc(sem["plain_out"], 1)
                    act.wait_ge(sem["w_used"], E.at("w_used", 12))
                    fn(qk[:, 8, :], bank(0), ACT.Copy).then_inc(sem["plain_out"], 1)
                    act.wait_ge(sem["w_used"], E.at("w_used", 16))
                    for b in range(TB):
                        fn(v_bc[:, b, :], bank(b, V_BC), ACT.Copy).then_inc(sem["plain_out"], 1)
                    act.wait_ge(sem["plain_out"], E.at("plain_out", 6))
                    fn(gates[:], v_bc[:, :, V_BC - GATES:V_BC], ACT.Sigmoid)
                elif kind == "proj_cq":
                    normed_blocks(ph, 0, 0, 4)
                elif kind == "proj_u":
                    for k in range(PIECES):
                        act.wait_ge(sem["w_used"], E.at("w_used", k + 1))
                        fn(qk[:, k, :], bank(k), ACT.Copy).then_inc(sem["plain_out"], 1)
                    act.wait_ge(sem["w_used"], E.at("w_used", 8))
                    fn(f_t[:, 0, :], psum[0:8, 4 * S:5 * S], ACT.Copy).then_inc(sem["plain_out"], 1)

            def attention(ph):
                units = units_of(ph.kind)
                n = len(units)
                extra = 1 if ph.kind == "att_b" else 0
                with E.loop(2) as it:
                    def exps(j):
                        half, i, br, lo, blocks = units[j % n]
                        w = CMP_N if br == "cmp" else blocks * P + extra
                        act.wait_ge(sem["row_max"], E.at("row_max", it * (2 * n) + j + 1))
                        fn(s_sb[:, j % 2, 0:w], s_sb[:, j % 2, 0:w], ACT.Exp, bias=neg_max[:, j % 2:j % 2 + 1],
                           accum_out=row_sum[:, j % 2:j % 2 + 1]).then_inc(sem["exps"], 1)

                    exps(0)
                    for j in range(2 * n):
                        if j + 1 < 2 * n:
                            exps(j + 1)
                        half, i, br, lo, blocks = units[j % n]
                        act.wait_ge(sem["transposed"], E.at("transposed", it * (2 * n) + j + 1))
                        if br == "cmp":
                            fn(pt_sb[0:CMP_N, j % 2, 0:P], psum[0:CMP_N, (2 + j % 2) * S:(2 + j % 2) * S + P],
                               ACT.Copy).then_inc(sem["pt_copied"], 1)
                        else:
                            fn(pt_sb[:, j % 2, 0:blocks * P], bank(2 + j % 2, blocks * P), ACT.Copy)\
                                .then_inc(sem["pt_copied"], 1)

            def compress(ph):
                act.dma_start(cmp_w[:], cmp_w1[0]).then_inc(sem["cmp_loaded"], 16)
                for kv in (0, 1):
                    act.wait_ge(sem["cmp_pe"], E.at("cmp_pe", 3 * kv + 1))
                    for hid in (0, 1):
                        ins = fn(cmp_h[:, hid, :], bank(hid, 2 * CMP_N), ACT.Gelu_apprx_tanh)
                    ins.then_inc(sem["cmp_act"], 1)
                    if kv == 0:
                        act.dma_start(cmp_w[:], cmp_w1[1]).then_inc(sem["cmp_loaded"], 16)
                        act.wait_ge(sem["cmp_pe"], E.at("cmp_pe", 2))
                        fn(cmp_s[:, 0, :], bank(2, CMP_N), ACT.Square).then_inc(sem["cmp_act"], 1)
                        act.wait_ge(sem["cmp_dve"], E.at("cmp_dve", 2))
                        fn(cmp_s[:, 0, :], cmp_s[:, 1, :], ACT.Sqrt).then_inc(sem["cmp_act"], 1)
                act.wait_ge(sem["cmp_pe"], E.at("cmp_pe", 5))
                fn(vc_sb[:], psum[0:CMP_N, 2 * S:2 * S + P], ACT.Copy).then_inc(sem["cmp_act"], 1)

            def split(ph):
                if ph.kind == "split1":
                    for j in range(4):
                        square(ph, j, branch[:, j, :])
                        if j:
                            root(ph, j - 1)
                    root(ph, 3)
                    act.wait_ge(sem["qk_out"], E.at("qk_out", 4))
                for c in range(12):
                    fn(br_hi[:, c, :], branch[:, c, :], ACT.Copy).then_inc(sem["br_hi"], 1)

            def merge(ph):
                for gi, g, r, par, first in groups_of(E, ph):
                    for n in range(3):
                        act.wait_ge(sem["w_used"], E.at("w_used", gi * PIECES + (12 * n + KC - 1) // 9 + 1))
                        if not first:
                            act.wait_ge(sem["y_read"], E.at("y_read", g * 3 + n - 2))
                        fn(sig_t[:, n, :], bank(2 * n), ACT.Sigmoid).then_inc(sem["gate_sig"], 1)

            def msplit(ph):
                for c in range(KC):
                    fn(h_hi[:, c, :], merged[:, c, :], ACT.Copy).then_inc(sem["h_hi"], 1)

            def ada_load(ph, gi, q, par):
                n = gi * 3 + q
                b = (par + q) % 2
                act.wait_ge(sem["ada_used"], E.at("ada_used", n - 1))
                act.nop(nofuse=True)
                base = E.turn * 12 + (START[ph.name]["ada_used"] - START["mlp_up"]["ada_used"] + n)
                act.dma_start(ada_t[:, b, :, :], ada[bass.ds(base, 1), :, :].rearrange("a p n -> p (a n)"))\
                    .then_inc(ada_loaded[b], 16)

            def up(ph):
                ffn = ph.kind == "ffn_up"
                per = 2 if ffn else 4
                func = ACT.Silu if ffn else ACT.Relu
                for gi, g, r, par, first in groups_of(E, ph):
                    def part(k):
                        act.wait_ge(sem["product"], E.at("product", g * per + k + 1))
                        act.nop(nofuse=True)
                        fn(row(a_hi, g * per + k), g_sb[:, k % 2, :], ACT.Copy)\
                            .then_inc(sem["act_hi"], 1)

                    for k in range(per):
                        if not ffn and k < 3:
                            ada_load(ph, gi, k, par)
                        act.wait_ge(sem["w_used"], E.at("w_used", gi * PIECES + (2 * k if ffn else k) + 1))
                        if not first or k >= 2:
                            act.wait_ge(sem["act_lo"], E.at("act_lo", g * per + (k - 1)))
                        fn(g_sb[:, k % 2, :], bank(2 * k if ffn else k), func).then_inc(sem["gated"], 1)
                        if k:
                            part(k - 1)
                    part(per - 1)

            def down(ph):
                if ph.name == "mlp_down":
                    for gi, g, r, par, first in groups_of(E, ph):
                        for q in range(3):
                            ada_load(ph, gi, q, par)

            def pool_mix(ph):
                act.wait_ge(sem["forget_dve"], E.at("forget_dve", 1))
                fn(f_t[:, 2, :], f_t[:, 1, :], ACT.Abs).then_inc(act_chain, 1)
                act.wait_ge(act_chain, E.step())
                fn(f_t[:, 2, :], f_t[:, 2, :], ACT.Exp, scale=-1.0).then_inc(sem["forget_step"], 1)
                act.wait_ge(sem["forget_step"], E.at("forget_step", 1))
                fn(f_t[:, 3, :], f_t[:, 2, :], ACT.Ln, bias=1.0).then_inc(sem["forget_step"], 1)
                for g in range(4):
                    act.wait_ge(sem["pool_mm"], E.at("pool_mm", g + 1))
                    fn(branch[:, 4 + g, :], bank(g % 2), ACT.Copy,
                       scale=lay[:, LY["pool_scale"] + g:LY["pool_scale"] + g + 1]).then_inc(sem["pool_out"], 1)
                act.wait_ge(sem["forget_dve"], E.at("forget_dve", 3))
                act.dma_start(cum_dram, f_t[:, 4, :]).then_inc(sem["cum_stored"], 16)
                act.wait_ge(sem["cum_stored"], E.at("cum_stored", 16))

            def run(ph):
                kind = ph.kind
                if kind == "prep":
                    act.wait_ge(sem["prep_loaded"], E.at("prep_loaded", 96))
                    fn(c_bcast, c_t[:], ACT.Silu).then_inc(sem["prep_step"], 1)
                    act.wait_ge(sem["prep_step"], E.at("prep_step", 4))
                    fn(lam_t[:, 2:4], lam_t[:, 0:2], ACT.Exp).then_inc(sem["prep_step"], 1)
                elif kind == "norm":
                    norm(ph)
                elif kind.startswith("proj"):
                    proj(ph)
                elif kind.startswith("att"):
                    attention(ph)
                elif kind == "compress":
                    compress(ph)
                elif kind.startswith("split"):
                    split(ph)
                elif kind == "merge":
                    merge(ph)
                elif kind == "msplit":
                    msplit(ph)
                elif kind.endswith("up"):
                    up(ph)
                elif kind == "down":
                    down(ph)
                elif kind == "pool":
                    pool_mix(ph)
                elif kind == "layer":
                    act.dma_start(lay[:], layer_small[bass.ds(E.turn, 1), :, :].rearrange("a p n -> p (a n)"))\
                        .then_inc(sem["layer_loaded"], 16)
                    act.wait_ge(sem["layer_loaded"], E.at("layer_loaded", 16))
                act.nop(nofuse=True)
                act.drain().then_inc(sem["phase_done"], 1)
                act.wait_ge(sem["phase_done"], E.at("phase_done", 3))

            walk(E, run)

        @block.vector
        def _(dve):
            E = Engine(dve, "dve")
            v = nc.vector
            dve.nop().then_inc(sem["ada_used"], PRESET["ada_used"])

            def col(t, c, n=1):
                return t[:, c:c + n]

            def norm(ph):
                name = ph.name
                if name in ("norm_mix", "norm_mlp"):
                    v.tensor_copy(norm_a[:], col(small, SM["mix" if name == "norm_mix" else "mlp"], KC)).then_inc(dve_chain, 1)
                    dve.wait_ge(dve_chain, E.step())
                    v.memset(norm_b[:], 0.0).then_inc(dve_chain, 1)
                    dve.wait_ge(dve_chain, E.step())
                    v.memset(res_scale[:], 1.0).then_inc(dve_chain, 1)
                    dve.wait_ge(dve_chain, E.step())
                else:
                    n = {"norma": 0, "norm_l": 1, "normb": 2}[name]
                    v.tensor_scalar(norm_b[:], col(mod, (3 * n + 1) * KC, KC), 1.0, None, ALU.add).then_inc(dve_chain, 1)
                    dve.wait_ge(dve_chain, E.step())
                    v.tensor_tensor(norm_a[:], norm_b[:], col(lay, LY["gain"] + n * KC, KC), ALU.mult).then_inc(dve_chain, 1)
                    dve.wait_ge(dve_chain, E.step())
                    v.tensor_copy(norm_b[:], col(mod, 3 * n * KC, KC)).then_inc(dve_chain, 1)
                    dve.wait_ge(dve_chain, E.step())
                    v.tensor_scalar(res_scale[:], col(mod, (3 * n + 2) * KC, KC), 1.0 if n == 1 else 0.5,
                                    None, ALU.mult).then_inc(dve_chain, 1)
                    dve.wait_ge(dve_chain, E.step())
                dve.wait_ge(sem["norm_summed"], E.at("norm_summed", KC))
                v.tensor_scalar(ninv[:], bank(4), 1.0 / D, EPS, ALU.mult, ALU.add).then_inc(dve_chain, 1)
                dve.wait_ge(dve_chain, E.step())
                v.reciprocal(ninv[:], ninv[:]).then_inc(sem["norm_inverse"], 1)

                def low(c):
                    dve.wait_ge(sem["h_hi"], E.at("h_hi", c + 1))
                    v.scalar_tensor_tensor(h_lo[:, c, :], nt[:, c % 2, :], norm_b[:, c:c + 1],
                                           h_hi[:, c, :].bitcast(F32), ALU.add, ALU.subtract).then_inc(dve_chain, 1)
                    dve.wait_ge(dve_chain, E.step())

                dve.wait_ge(sem["norm_rstd"], E.at("norm_rstd", 1))
                for c in range(KC):
                    v.scalar_tensor_tensor(nt[:, c % 2, :], x[:, c, :], norm_a[:, c:c + 1], nrs[:],
                                           ALU.mult, ALU.mult).then_inc(sem["norm_scaled"], 1)
                    if c:
                        low(c - 1)
                low(KC - 1)

            def inverse(ph, j, dim):
                dve.wait_ge(sem["qk_summed"], E.at("qk_summed", j + 1))
                v.tensor_scalar(inv_t[:, j % 2, :], bank(4 + j % 2), 1.0 / dim, EPS, ALU.mult, ALU.add).then_inc(dve_chain, 1)
                dve.wait_ge(dve_chain, E.step())
                v.reciprocal(inv_t[:, j % 2, :], inv_t[:, j % 2, :]).then_inc(sem["qk_inverse"], 1)

            def proj(ph):
                kind = ph.kind
                if kind == "proj_u":
                    return
                gain, where = dict(
                    proj_a=([(small, SM["gain"] + 0)] * 4 + [(small, SM["gain"] + 1)] * 4, range(8)),
                    proj_a2=([(lay, LY["qk"] + 0)] * 4 + [(lay, LY["qk"] + 1)] * 4, range(8)),
                    proj_c2=([(lay, LY["qk"] + 2)] * 4 + [(lay, LY["qk"] + 3)] * 4, range(8)),
                    proj_bc=([(small, SM["gain"] + 2)] * 4 + [(small, SM["gain"] + n) for n in (3, 6, 7)],
                             range(7)),
                    proj_cq=([(small, SM["gain"] + 4)] * 4, range(4)),
                )[kind]

                def finish(j):
                    t, c = gain[j]
                    dve.wait_ge(sem["qk_rstd"], E.at("qk_rstd", j + 1))
                    if j < 4:
                        v.tensor_scalar(rs_t[:, j % 2, :], rs_t[:, j % 2, :], 0.125, None, ALU.mult).then_inc(dve_chain, 1)
                        dve.wait_ge(dve_chain, E.step())
                    v.scalar_tensor_tensor(qk[:, where[j], :], bank(j % 4), t[:, c:c + 1], rs_t[:, j % 2, :],
                                           ALU.mult, ALU.mult).then_inc(sem["qk_out"], 1)

                for j in range(len(gain)):
                    inverse(ph, j, HALF)
                    if j:
                        finish(j - 1)
                finish(len(gain) - 1)

            def attention(ph):
                kind = ph.kind
                units = units_of(kind)
                n = len(units)
                with E.loop(2) as it:
                    def maxima(j):
                        u, (half, i, br, lo, blocks) = j // n, units[j % n]
                        pb = j % 2
                        if j % n == 0:
                            dve.wait_ge(bias_loaded[u], E.at(f"bias{u}", (it + 1) * (16 * TILES[kind])))
                            dve.nop(nofuse=True)
                        if j >= 2:
                            dve.wait_ge(sem["transposed"], E.at("transposed", it * (2 * n) + (j - 1)))
                            dve.nop(nofuse=True)
                        first = -3e38
                        if kind == "att_b":
                            w = blocks * P
                            v.tensor_copy(s_sb[:, pb, w:w + 1],
                                          small[:, bass.ds(it * 4 + (SM["sinks"] + 2 * u + half), 1)]).then_inc(dve_chain, 1)
                            dve.wait_ge(dve_chain, E.step())
                            first = s_sb[:, pb, w:w + 1]
                        dve.wait_ge(sem["scores"], E.at("scores", it * (2 * n) + j + 1))
                        dve.nop(nofuse=True)
                        if br == "cmp":
                            c = CS["cmask"] + i * CMP_N
                            w, tile = CMP_N, cst[:, c:c + CMP_N]
                        else:
                            w = blocks * P
                            t = half if TILES[kind] == 2 else 0
                            c = 0 if kind == "att_c2" else (TB - 1 - i + lo) * P
                            tile = bias_t[:, u, t, c:c + w]
                        v.tensor_tensor_reduce(out=s_sb[:, pb, 0:w], in0=bank(pb, w), in1=tile, scale=1.0,
                                               scalar=first, op0=ALU.add, op1=ALU.max,
                                               accum_out=row_max[:, pb:pb + 1]).then_inc(dve_chain, 1)
                        dve.wait_ge(dve_chain, E.step())
                        v.tensor_scalar(neg_max[:, pb:pb + 1], row_max[:, pb:pb + 1], -1.0, None, ALU.mult)\
                            .then_inc(sem["row_max"], 1)

                    def write_out(u):
                        dve.wait_ge(sem["pv"], E.at("pv", it * (2 * n) + (u + 1) * n))
                        dve.nop(nofuse=True)
                        b = dict(att_a=0, att_b=4, att_c=8, att_a2=0, att_c2=8)[kind]
                        v.tensor_copy(row(branch, it * 2 + (b + u)), bank(4 + u))\
                            .then_inc(sem["pair_done"], 1)

                    maxima(0)
                    for j in range(2 * n):
                        if j + 1 < 2 * n:
                            maxima(j + 1)
                        u, (half, i, br, lo, blocks) = j // n, units[j % n]
                        pb = j % 2
                        w = CMP_N if br == "cmp" else blocks * P
                        dve.wait_ge(sem["exps"], E.at("exps", it * (2 * n) + j + 1))
                        v.reciprocal(row_inv[:, pb:pb + 1], row_sum[:, pb:pb + 1]).then_inc(dve_chain, 1)
                        dve.wait_ge(dve_chain, E.step())
                        factor = row_inv[:, pb:pb + 1]
                        if kind == "att_a" and half == 1:
                            v.tensor_tensor(row_scale[:, pb:pb + 1], factor, neg_lam[:], ALU.mult).then_inc(dve_chain, 1)
                            dve.wait_ge(dve_chain, E.step())
                            factor = row_scale[:, pb:pb + 1]
                        if kind == "att_c":
                            c = 3 * half + {"cmp": 0, "sel": 1, "win": 2}[br]
                            v.tensor_tensor(row_scale[:, pb:pb + 1], factor,
                                            gates[:, i, bass.ds(it * 12 + (6 * u + c), 1)], ALU.mult).then_inc(dve_chain, 1)
                            dve.wait_ge(dve_chain, E.step())
                            factor = row_scale[:, pb:pb + 1]
                            if br == "cmp" and i == 0:
                                v.tensor_tensor(factor, factor, cst[:, CS["valid"]:CS["valid"] + 1], ALU.mult).then_inc(dve_chain, 1)
                                dve.wait_ge(dve_chain, E.step())
                        v.tensor_scalar(s_sb[:, pb, 0:w], s_sb[:, pb, 0:w], factor, None, ALU.mult)\
                            .then_inc(sem["probs"], 1)
                        if j == n + 1:
                            write_out(0)
                    write_out(1)

            def compress(ph):
                for kv in (0, 1):
                    src = qk[:, 7 + kv, :]
                    if kv:
                        dve.wait_ge(sem["cmp_pe"], E.at("cmp_pe", 1))
                    for half in (0, 1):
                        for g in (0, 1):
                            v.tensor_copy(cmp_t[half * HALF:(half + 1) * HALF, g, 0:S - 1],
                                          src[g * HALF:(g + 1) * HALF, half:half + S - 1]).then_inc(dve_chain, 1)
                            dve.wait_ge(dve_chain, E.step())
                    pos = small[:, SM["pos"] + kv * CMP_STRIDE:SM["pos"] + (kv + 1) * CMP_STRIDE]
                    for g in (0, 1):
                        for part in (0, 1):
                            a = cmp_t[:, g, 16 * part:16 * part + CMP_N * 16]\
                                .rearrange("p (c j t) -> p j t c", j=8, t=2)[:, :, 0, :]
                            v.tensor_tensor(cmp_x[:, 8 * part:8 * part + 8, g, :], a,
                                            pos[:, 8 * part:8 * part + 8].unsqueeze(2).to_broadcast([P, 8, CMP_N]),
                                            ALU.add).then_inc(dve_chain, 1)
                            dve.wait_ge(dve_chain, E.step())
                    v.tensor_scalar(tiny_t[:], ones[:, 0:1], 1.0, None, ALU.mult).then_inc(sem["cmp_dve"], 1)
                    if kv == 0:
                        dve.wait_ge(sem["cmp_pe"], E.at("cmp_pe", 3))
                        v.tensor_scalar(cmp_s[:, 1, :], bank(3, CMP_N), 1.0 / HALF, EPS, ALU.mult, ALU.add).then_inc(dve_chain, 1)
                        dve.wait_ge(dve_chain, E.step())
                        v.reciprocal(cmp_s[:, 1, :], cmp_s[:, 1, :]).then_inc(sem["cmp_dve"], 1)
                        dve.wait_ge(sem["cmp_act"], E.at("cmp_act", 3))
                        v.scalar_tensor_tensor(kc_sb[:], bank(2, CMP_N), col(small, SM["gain"] + 5),
                                               cmp_s[:, 0, :], ALU.mult, ALU.mult).then_inc(sem["cmp_dve"], 1)

            def split(ph):
                if ph.kind == "split1":
                    def finish(j):
                        dve.wait_ge(sem["qk_rstd"], E.at("qk_rstd", j + 1))
                        v.scalar_tensor_tensor(branch[:, j, :], branch[:, j, :], col(small, SM["subln"]),
                                               rs_t[:, j % 2, :], ALU.mult, ALU.mult).then_inc(dve_chain, 1)
                        dve.wait_ge(dve_chain, E.step())
                        v.tensor_scalar(branch[:, j, :], branch[:, j, :], 1.0 - LAM_INIT, None, ALU.mult)\
                            .then_inc(sem["qk_out"], 1)

                    for j in range(4):
                        inverse(ph, j, P)
                        if j:
                            finish(j - 1)
                    finish(3)
                    dve.wait_ge(sem["qk_out"], E.at("qk_out", 4))
                for c in range(12):
                    dve.wait_ge(sem["br_hi"], E.at("br_hi", c + 1))
                    v.tensor_tensor(br_lo[:, c, :], branch[:, c, :], br_hi[:, c, :].bitcast(F32), ALU.subtract)

            def merge(ph):
                for gi, g, r, par, first in groups_of(E, ph):
                    m = row(merged, g)
                    for n in range(3):
                        dve.wait_ge(sem["gate_sig"], E.at("gate_sig", g * 3 + n + 1))
                        dve.wait_ge(sem["w_used"], E.at("w_used", gi * PIECES + (12 * n + 11) // 9 + 1))
                        dst = m if n == 0 else prod_t[:]
                        ins = v.tensor_tensor(dst, sig_t[:, n, :], bank(2 * n + 1), ALU.mult)
                        ins.then_inc(sem["y_read"], 1)
                        if n:
                            dve.wait_ge(sem["y_read"], E.at("y_read", g * 3 + n + 1))
                            v.tensor_tensor(m, m, prod_t[:], ALU.add).then_inc(dve_chain, 1)
                            dve.wait_ge(dve_chain, E.step())

            def msplit(ph):
                for c in range(KC):
                    dve.wait_ge(sem["h_hi"], E.at("h_hi", c + 1))
                    v.tensor_tensor(h_lo[:, c, :], merged[:, c, :], h_hi[:, c, :].bitcast(F32), ALU.subtract)

            def ada_sum(ph, gi, q, par):
                b = (par + q) % 2
                n = gi * 3 + q
                before = START[ph.name].get(f"ada{b}", 0)
                count = (n // 2 + 1) * 16
                dve.wait_ge(ada_loaded[b], E.at(f"ada{b}", count))
                dve.nop(nofuse=True)
                for t in range(ADA):
                    ins = v.tensor_tensor_reduce(out=ada_junk, in0=ada_t[:, b, t, :], in1=c_bcast, scale=1.0,
                                                 scalar=0.0, op0=ALU.mult, op1=ALU.add,
                                                 accum_out=mod_part[:, 3 * q + t:3 * q + t + 1])
                    if t < ADA - 1:
                        ins.then_inc(dve_chain, 1)
                        dve.wait_ge(dve_chain, E.step())
                    else:
                        ins.then_inc(sem["ada_used"], 1)
                        dve.wait_ge(sem["ada_used"], E.at("ada_used", n + 1))
                if q == 2:
                    at0 = 9 * gi + (0 if ph.name == "mlp_up" else 18)
                    v.tensor_copy(mods[:, bass.ds(E.turn * 36 + at0, 9)], mod_part[:]).then_inc(dve_chain, 1)
                    dve.wait_ge(dve_chain, E.step())

            def up(ph):
                ffn = ph.kind == "ffn_up"
                per = 2 if ffn else 4
                for gi, g, r, par, first in groups_of(E, ph):
                    def low(k):
                        dve.wait_ge(sem["act_hi"], E.at("act_hi", g * per + k + 1))
                        v.tensor_tensor(row(a_lo, g * per + k), g_sb[:, k % 2, :],
                                        row(a_hi, g * per + k).bitcast(F32), ALU.subtract)\
                            .then_inc(sem["act_lo"], 1)

                    for k in range(per):
                        dve.wait_ge(sem["gated"], E.at("gated", g * per + k + 1))
                        dve.wait_ge(sem["w_used"], E.at("w_used", gi * PIECES + (2 * k + 1 if ffn else k) + 1))
                        v.tensor_tensor(g_sb[:, k % 2, :], g_sb[:, k % 2, :], bank(2 * k + 1 if ffn else k),
                                        ALU.mult).then_inc(sem["product"], 1)
                        if not ffn and k < 3:
                            ada_sum(ph, gi, k, par)
                        if k:
                            low(k - 1)
                    low(per - 1)

            def down(ph):
                for gi, g, r, par, first in groups_of(E, ph):
                    for k in range(PIECES):
                        dve.wait_ge(sem["w_used"], E.at("w_used", gi * PIECES + k + 1))
                        xc = x[:, 4 * g + k, :]
                        v.scalar_tensor_tensor(xc, bank(k), res_scale[:, 4 * g + k:4 * g + k + 1], xc,
                                               ALU.mult, ALU.add).then_inc(sem["x_added"], 1)
                        if ph.name == "mlp_down" and k < 3:
                            ada_sum(ph, gi, k, par)

            def pool_mix(ph):
                f0 = f_t[:, 0, :]
                v.tensor_scalar(f_t[:, 1, :], f0, lay[0:8, LY["f_bias"]:LY["f_bias"] + 1], None, ALU.add)\
                    .then_inc(sem["forget_dve"], 1)
                for g in range(4):
                    src, n = qk[:, g, :], 0
                    for step in range(g + 1):
                        sh, dst = 2 ** step, pool_s[:, step % 2, :]
                        v.tensor_copy(dst[:, 0:sh], src[:, 0:sh]).then_inc(dve_chain, 1)
                        dve.wait_ge(dve_chain, E.step())
                        v.tensor_tensor(dst[:, sh:S], src[:, sh:S], src[:, 0:S - sh], ALU.add).then_inc(dve_chain, 1)
                        dve.wait_ge(dve_chain, E.step())
                        src = dst
                    w = CS["inv_count"] + 16 * g
                    v.tensor_tensor(src[:, 0:16], src[:, 0:16], cst[:, w:w + 16], ALU.mult).then_inc(dve_chain, 1)
                    dve.wait_ge(dve_chain, E.step())
                    v.tensor_scalar(src[:, 16:S], src[:, 16:S], 1.0 / 2 ** (g + 1), None, ALU.mult).then_inc(dve_chain, 1)
                    dve.wait_ge(dve_chain, E.step())
                    if g:
                        dve.wait_ge(sem["pool_mm"], E.at("pool_mm", g))
                    v.tensor_tensor(pool_d[:], src, qk[:, g, :], ALU.subtract).then_inc(sem["pool_in"], 1)
                    dve.wait_ge(sem["pool_in"], E.at("pool_in", g + 1))
                dve.wait_ge(sem["forget_dve"], E.at("forget_dve", 1))
                v.tensor_scalar(f_t[:, 0, :], f_t[:, 1, :], 0.0, None, ALU.min).then_inc(dve_chain, 1)
                dve.wait_ge(dve_chain, E.step())
                dve.wait_ge(sem["forget_step"], E.at("forget_step", 2))
                v.tensor_tensor(f_t[:, 0, :], f_t[:, 3, :], f_t[:, 0, :], ALU.subtract).then_inc(dve_chain, 1)
                dve.wait_ge(dve_chain, E.step())
                v.memset(f_t[:, 1, :], 1.0).then_inc(dve_chain, 1)
                dve.wait_ge(dve_chain, E.step())
                v.tensor_tensor_scan(f_t[:, 4, :], f_t[:, 1, :], f_t[:, 0, :], 0.0, ALU.mult, ALU.add)\
                    .then_inc(sem["forget_dve"], 2)

            def prep(ph):
                dve.wait_ge(sem["prep_loaded"], E.at("prep_loaded", 96))
                for n in (0, 1):
                    v.tensor_tensor_reduce(out=rs_t[:, n, 0:HALF], in0=lam_w[:, 2 * n, :],
                                           in1=lam_w[:, 2 * n + 1, :], scale=1.0, scalar=0.0, op0=ALU.mult,
                                           op1=ALU.add, accum_out=lam_t[:, n:n + 1]).then_inc(sem["prep_step"], 1)
                dve.wait_ge(sem["prep_step"], E.at("prep_step", 5))
                v.tensor_tensor(neg_lam[:], lam_t[:, 3:4], lam_t[:, 2:3], ALU.subtract).then_inc(dve_chain, 1)
                dve.wait_ge(dve_chain, E.step())
                v.tensor_scalar(neg_lam[:], neg_lam[:], -LAM_INIT, None, ALU.add).then_inc(dve_chain, 1)
                dve.wait_ge(dve_chain, E.step())

            def run(ph):
                kind = ph.kind
                if kind == "prep":
                    prep(ph)
                elif kind == "norm":
                    norm(ph)
                elif kind.startswith("proj"):
                    proj(ph)
                elif kind.startswith("att"):
                    attention(ph)
                elif kind == "compress":
                    compress(ph)
                elif kind.startswith("split"):
                    split(ph)
                elif kind == "merge":
                    merge(ph)
                elif kind == "msplit":
                    msplit(ph)
                elif kind.endswith("up"):
                    up(ph)
                elif kind == "down":
                    down(ph)
                elif kind == "pool":
                    pool_mix(ph)
                elif kind == "layer":
                    dve.wait_ge(sem["layer_loaded"], E.at("layer_loaded", 16))
                    dve.nop(nofuse=True)
                    v.tensor_copy(mod[:], mods[:, bass.ds(E.turn * MODS, MODS)]).then_inc(dve_chain, 1)
                    dve.wait_ge(dve_chain, E.step())
                    v.tensor_tensor(mod[:], mod[:], col(lay, LY["b_ada"], MODS), ALU.add).then_inc(dve_chain, 1)
                    dve.wait_ge(dve_chain, E.step())
                dve.nop(nofuse=True)
                dve.drain().then_inc(sem["phase_done"], 1)
                dve.wait_ge(sem["phase_done"], E.at("phase_done", 3))

            walk(E, run)


def tiles_of(w):
    k, n = w.shape
    return w.reshape(k // P, P, n).transpose(1, 0, 2).reshape(P, -1)


def stream(groups):
    return np.concatenate([np.concatenate(g, axis=1).ravel() for g in groups])


def blocks_of(w, n):
    return [tiles_of(w[:, P * i:P * (i + 1)]) for i in range(n)]


def fours(blocks):
    return [blocks[i:i + 4] for i in range(0, len(blocks), 4)]


def mix_groups(w_gate, w_branch, w_out):
    out = []
    for d in range(KC):
        g = []
        for n in range(3):
            g.append(tiles_of(w_gate[:, n * D + d * P:n * D + (d + 1) * P]))
            g.append(tiles_of(w_branch[n][:, d * P:(d + 1) * P]))
        out.append(g)
    return out + fours(blocks_of(w_out, KC))


def bucket(dist):
    n = np.maximum(dist, 0)
    large = 16 + (np.log(np.maximum(n, 1).astype(np.float32) / np.float32(16)) / np.float32(np.log(8.0))
                  * np.float32(16)).astype(np.int32)
    return np.where(n < 16, n, np.minimum(large, 31))


def kernel(x, w_in, qk_gain, diff_lambda, diff_subln, sinks, cmp_pos, cmp_w1, cmp_w2, w_branch, w_out,
           norm_mix, norm_mlp, w_up, w_down, rel_bias, c_2, w_ada_2, b_ada_2, norm_gain_2,
           ffn_w_gate_2, ffn_w_up_2, ffn_w_down_2, w_in_2, qk_gain_2, rel_bias_2, forget_bias_2,
           w_pool_2, pool_scale_2, w_branch_2, w_out_2):
    import concourse.bacc as bacc
    from concourse.bass_utils import run_bass_kernel_spmd

    arr = np.ascontiguousarray
    (x, w_in, qk_gain, diff_lambda, diff_subln, sinks, cmp_pos, cmp_w1, cmp_w2, w_branch, w_out, norm_mix,
     norm_mlp, w_up, w_down, rel_bias, c_2, w_ada_2, b_ada_2, norm_gain_2, ffn_w_gate_2, ffn_w_up_2,
     ffn_w_down_2, w_in_2, qk_gain_2, rel_bias_2, forget_bias_2, w_pool_2, pool_scale_2, w_branch_2,
     w_out_2) = map(np.asarray, (
         x, w_in, qk_gain, diff_lambda, diff_subln, sinks, cmp_pos, cmp_w1, cmp_w2, w_branch, w_out,
         norm_mix, norm_mlp, w_up, w_down, rel_bias, c_2, w_ada_2, b_ada_2, norm_gain_2, ffn_w_gate_2,
         ffn_w_up_2, ffn_w_down_2, w_in_2, qk_gain_2, rel_bias_2, forget_bias_2, w_pool_2,
         pool_scale_2, w_branch_2, w_out_2))

    heads = np.array([g * 4 + r for r in range(4) for g in range(2)])
    by_pair = (heads[:, None] * HALF + np.arange(HALF)).ravel()
    w = w_in[0]
    ends = np.cumsum([512, 512, 512, 512, 128, 128, 512, 768, 24, 3072])
    aq, ak, av, bq, bk, bv, cq, ckv, cg, mg = np.split(w, ends[:-1], axis=1)
    ck = [ckv[:, i * P:(i + 1) * P] for i in range(6)]
    cg = cg.reshape(D, 8, 3)[:, heads].reshape(D, GATES)
    wb = [w_branch[0, 0], w_branch[0, 1][by_pair], w_branch[0, 2][by_pair]]
    first = [blocks_of(aq, 4), blocks_of(ak, 4), [tiles_of(av)],
             blocks_of(bq[:, by_pair], 4), [tiles_of(t) for t in (bk, ck[2], ck[4], ck[0])], [tiles_of(ck[1])],
             [tiles_of(np.concatenate([bv, ck[3], ck[5], cg], axis=1))],
             blocks_of(cq[:, by_pair], 4)] + mix_groups(mg, wb, w_out[0])
    mlp = []
    for m in range(4):
        part = slice(m * D, (m + 1) * D)
        mlp += fours(blocks_of(w_up[0][:, part], 8)) + fours(blocks_of(w_down[0][part], 8))

    def ffn(l, n):
        out, at = [], 0
        for chunks in FFN_PARTS:
            part = slice(at * P, (at + chunks) * P)
            gate, up = (blocks_of(t[l, n][:, part], chunks) for t in (ffn_w_gate_2, ffn_w_up_2))
            out += [[gate[i], up[i], gate[i + 1], up[i + 1]] for i in range(0, chunks, 2)]
            out += fours(blocks_of(ffn_w_down_2[l, n][part], 8))
            at += chunks
        return out

    layers = []
    for l in range(2):
        qa, ka, va, ub, qc, kc, vc, f, g = np.split(w_in_2[l], np.cumsum([512] * 7 + [8]), axis=1)
        f = np.concatenate([f, np.zeros((D, P - 8), f.dtype)], axis=1)
        layers += ffn(l, 0) + [blocks_of(qa, 4), blocks_of(ka, 4), [tiles_of(va)], blocks_of(ub, 4),
                               [tiles_of(f)], blocks_of(qc, 4), blocks_of(kc, 4), [tiles_of(vc)]]
        layers += mix_groups(g, w_branch_2[l], w_out_2[l]) + ffn(l, 1)

    def cols(v):
        return v.reshape(-1, P).T

    def both(v):
        return np.concatenate([v.T, v.T], axis=0)

    pos = cmp_pos[0].reshape(2, CMP_STRIDE, 2, HALF).transpose(2, 3, 0, 1).reshape(P, 2 * CMP_STRIDE)
    w2 = cmp_w2[0].reshape(2, 2, P, HALF).transpose(2, 0, 1, 3).reshape(P, 4 * HALF)
    small = np.concatenate([cols(norm_mix[0]), cols(norm_mlp[0]), both(qk_gain[0]), diff_subln[0][:, None],
                            np.broadcast_to(sinks[0][heads], (P, 8)), pos, w2], axis=1)
    lay = []
    for l in range(2):
        fb = np.concatenate([forget_bias_2[l], np.zeros(P - 8, np.float32)])[:, None]
        lay.append(np.concatenate([cols(norm_gain_2[l].ravel()), cols(b_ada_2[l]),
                                   w_pool_2[l].transpose(1, 0, 2).reshape(P, 4 * P), cols(pool_scale_2[l]),
                                   both(qk_gain_2[l]), fb], axis=1))
    dist = 384 + np.arange(P)[:, None] - np.arange(S)[None, :]
    b1 = rel_bias[bucket(dist)].transpose(2, 0, 1)
    b1 = b1[np.concatenate([np.arange(4), 4 + heads, 12 + heads])]
    b2 = rel_bias_2[:, :, np.clip(dist, -128, 128) + 128].reshape(16, P, S)
    w1 = cmp_w1[0].reshape(2, CMP_STRIDE, P, 2 * P).transpose(0, 2, 1, 3)
    ada = w_ada_2.transpose(0, 2, 1).reshape(48, ADA, P, D).transpose(0, 2, 1, 3).reshape(48, P, ADA * D)

    i, j = np.arange(P)[:, None], np.arange(P)[None, :]
    c, t = np.arange(CMP_N)[None, None, :], np.arange(S).reshape(TB, P).T[:, :, None]
    consts = np.concatenate([
        i == j, i // HALF == j // HALF, np.where(j > i, NEG, 0), np.where(j <= i, NEG, 0),
        np.where((i < HALF) & (j >= HALF), NEG, 0),
        np.where(c * CMP_STRIDE + 31 <= t, 0, NEG).reshape(P, TB * CMP_N), i >= 31,
        np.broadcast_to(1.0 / np.minimum(np.arange(16)[None, :] + 1, 2.0 ** np.arange(1, 5)[:, None]).reshape(1, 64),
                        (P, 64))], axis=1).astype(np.float32)

    ins = dict(
        x_in=x[0].T.reshape(KC, P, S).transpose(1, 0, 2), w_first=stream(first), w_mlp=stream(mlp),
        w_layer=stream(layers), ada=ada, first_small=small, layer_small=np.stack(lay),
        biases=np.concatenate([b1, b2]), cmp_w1=w1,
        lam_in=np.broadcast_to(diff_lambda[0], (P, 4, HALF)), c_in=np.broadcast_to(c_2, (P, D)), consts=consts)
    ins = {k: arr(v) for k, v in ins.items()}
    nc = bacc.Bacc("TRN2", target_bir_lowering=False, num_devices=1)
    aps = {k: nc.dram_tensor(k + "_dram", v.shape, F32, kind="ExternalInput").ap() for k, v in ins.items()}
    out = nc.dram_tensor("out_dram", (P, KC, S), F32, kind="ExternalOutput").ap()
    build(nc, *aps.values(), out)
    r = run_bass_kernel_spmd(nc, [{k + "_dram": v for k, v in ins.items()}], core_ids=[0])
    got = r.results[0]["out_dram"]
    return arr(got.transpose(1, 0, 2).reshape(D, S).T)[None]
```

```python
import numpy as np
import concourse.bass as bass
from concourse import mybir
from contextlib import ExitStack, contextmanager

F32 = mybir.dt.float32
F32R = mybir.dt.float32r
ACT = mybir.ActivationFunctionType
ALU = mybir.AluOpType

P = 128
S = 512
D = 1024
KC = D // P
TB = S // P
EPS = 1e-6
PIECES = 4
HALF = 64
CMP_N = 31
CMP_STRIDE = 16
NEG = -1e30
LAM_INIT = 0.2
V_BC = 408
SLOT = KC * P
MIX_TILES = KC + 4
DEPTH = 4
RAW = PIECES * SLOT
MODS = 72
GATES = 24
ADA = 3
FFN_PARTS = (8, 8, 6)
UNITS = dict(att_a=8, att_b=8, att_c=24, att_a2=8, att_c2=8)
TILES = dict(att_a=1, att_b=2, att_c=2, att_a2=2, att_c2=2)
SM = dict(mix=0, mlp=8, gain=16, subln=24, sinks=25, pos=33, w2=65)
SM_N = 65 + 2 * 2 * HALF
LY = dict(gain=0, b_ada=24, pool=96, pool_scale=608, qk=612, f_bias=616)
LY_N = 617
CS = dict(ident=0, pair_ones=128, tri=256, window=384, chunk=512, cmask=640, valid=764, inv_count=765)
CS_N = 765 + 64


ROOTS = dict(model=(1 / D, EPS), query=(1.0, HALF * EPS), key=(1 / HALF, EPS),
             differential=(1 / (P * (1 - LAM_INIT) ** 2), EPS / (1 - LAM_INIT) ** 2))


class Phase:

    def __init__(self, name, kind, groups=(), meets=True, **totals):
        self.meets = meets
        self.name, self.kind, self.groups, self.totals = name, kind, list(groups), dict(totals)
        n = sum(g for g, _ in self.groups)
        self.totals.update(w_hi=PIECES * n, w_lo=PIECES * n, w_used=PIECES * n, group=n, phase_done=3 * meets)
        self.floats = sum(g * PIECES * f * P for g, f in self.groups)


SUMMED_BEFORE = ("norm_mlp", "norm_l", "normb")
SUMMING = ("wout1", "downa2", "wout2")


def norm_phase(name):
    return Phase(name, "norm", meets=False, norm_root=1, norm_scaled=KC, h_hi=KC, h_lo=KC,
               **({} if name in SUMMED_BEFORE else dict(norm_squared=KC, norm_summed=KC)))


def attention_phase(kind):
    n = 4 * UNITS[kind]
    return Phase(kind, kind, scores=n, row_max=n, exps=n, probs=n, transposed=n, pt_copied=n,
                 pv=n, pair_done=4, staged=4, bias0=32 * TILES[kind], bias1=32 * TILES[kind],
                 v_staged=0 if kind in ("att_b", "att_c") else 4, bias_masked=0 if kind == "att_c2" else 4)


def proj_phase(name, groups, normed, plain):
    return Phase(name, name, groups, qk_squared=normed, qk_summed=normed, qk_inverse=normed,
                 qk_rstd=normed, qk_out=normed, plain_out=plain)


def up_phase(name, kind, groups, blocks):
    return Phase(name, kind, [(groups, KC * P)], gated=blocks, product=blocks, act_hi=blocks, act_lo=blocks)


def down_phase(name, tiles):
    sums = dict(norm_squared=KC, norm_summed=KC) if name in SUMMING else {}
    return Phase(name, "down", [(2, tiles * P)], x_added=KC, **sums)


def mix_phases(tag):
    return [
        Phase("split" + tag, "split" + tag, meets=False, br_hi=12, br_lo=12,
              **(dict(qk_squared=4, qk_summed=4, qk_inverse=4, qk_rstd=4, qk_out=4) if tag == "1" else {})),
        Phase("merge" + tag, "merge", [(3 * KC, MIX_TILES // PIECES * P)], gate_sig=3 * KC, y_read=3 * KC),
        Phase("msplit" + tag, "msplit", meets=False, h_hi=KC, h_lo=KC),
        down_phase("wout" + tag, KC),
    ]


def ffn_phases(tag):
    out = [norm_phase("norm" + tag)]
    for n, chunks in enumerate(FFN_PARTS):
        out += [up_phase(f"up{tag}{n}", "ffn_up", chunks // 2, chunks), down_phase(f"down{tag}{n}", chunks)]
    return out


FULL = KC * P
FIRST = ([Phase("prep", "prep", pair_done=2, prep_loaded=80, prep_step=4), norm_phase("norm_mix"),
          proj_phase("proj_a", [(3, FULL)], 8, 4), attention_phase("att_a"),
          proj_phase("proj_bc", [(2, FULL), (1, 2 * P), (1, 2 * V_BC)], 7, 6), attention_phase("att_b"),
          proj_phase("proj_cq", [(1, FULL)], 4, 0),
          Phase("compress", "compress", cmp_loaded=32, cmp_pe=5, cmp_dve=4, cmp_act=5), attention_phase("att_c")]
         + mix_phases("1") + [Phase("cond", "cond", layer_loaded=16), norm_phase("norm_mlp")])
MLP = [up_phase("mlp_up", "mlp_up", 2, 8), down_phase("mlp_down", KC)]
LAYER = ([Phase("layer", "layer", layer_loaded=32)] + ffn_phases("a")
         + [norm_phase("norm_l"),
            proj_phase("proj_a2", [(3, FULL)], 8, 4), attention_phase("att_a2"),
            proj_phase("proj_u", [(1, FULL), (1, 2 * P)], 0, 5),
            Phase("pool", "pool", pool_in=4, pool_mm=4, pool_out=4, forget_step=2, forget_dve=3, cum_stored=16),
            proj_phase("proj_c2", [(3, FULL)], 8, 4), attention_phase("att_c2")]
         + mix_phases("2") + ffn_phases("b"))
ADA_LOADS = dict(mlp_up=range(0, 2), mlp_down=range(2, 4), upa0=range(0, 4), downa0=range(4, 6),
                 upa1=range(6, 10), downa1=range(10, 12), upa2=range(12, 15), downa2=range(15, 16))
for ph in MLP + LAYER:
    if ph.name in ADA_LOADS:
        loads = ADA_LOADS[ph.name]
        ph.totals.update(ada0=16 * sum(n % 2 == 0 for n in loads), ada1=16 * sum(n % 2 for n in loads),
                         ada_used=len(loads))
SEGMENTS = [("first", FIRST, 1), ("mlp", MLP, 4), ("layer", LAYER, 2)]
PRESET = dict(w_lo=2 * PIECES, w_used=PIECES, ada_used=2)


def starts():
    at, per, now = {}, {}, dict(PRESET)
    for seg, phases, turns in SEGMENTS:
        entry = dict(now)
        for ph in phases:
            at[ph.name] = dict(now)
            for name, n in ph.totals.items():
                now[name] = now.get(name, 0) + n
        per[seg] = {name: n - entry.get(name, 0) for name, n in now.items()}
        assert turns == 1 or per[seg]["group"] % 2 == 0
        for name, n in per[seg].items():
            now[name] += n * (turns - 1)
    return at, per


START, PER = starts()
SEMS = sorted({s for _, phases, _ in SEGMENTS for ph in phases for s in ph.totals} - {"group"})

CHAIN = {'pool0': 2, 'pool1': 6, 'pool2': 2, 'pool6': 4, 'pool7': 2, 'act5': 1, 'dve0': 40, 'dve1': 48, 'dve2': 148, 'dve3': 2, 'dve4': 12, 'dve6': 32, 'dve7': 32, 'dve8': 2, 'dve5': 240, 'pool5': 12}
WANTED = {}


class Engine:

    def __init__(self, eng, name):
        self.e, self.name = eng, name
        self.phase = None
        self.seg, self.turn = "first", None
        self.base, self.n, self.loops = 0, 0, 0

    def at(self, sem, more):
        v = START[self.phase].get(sem, 0)
        per = PER[self.seg].get(sem, 0)
        if self.turn is not None and per:
            return self.turn * per + (more + v)
        return more + v

    def step(self):
        self.n += 1
        return self.base + self.n

    @contextmanager
    def loop(self, turns):
        key = f"{self.name}{self.loops}"
        self.loops += 1
        per = CHAIN.get(key, 0)
        base, n = self.base, self.n
        self.e.nop(nofuse=True)
        with self.e.Fori(0, turns) as it:
            if per:
                self.base = it * per + base
            yield it
        if self.n - n != per:
            WANTED[key] = self.n - n
        self.base, self.n = base, n + turns * per

    @contextmanager
    def segment(self, name, turns):
        with self.loop(turns) as it:
            self.seg, self.turn = name, it
            yield it
        self.seg, self.turn = "first", None


def walk(E, run):
    def phases(part):
        for ph in part:
            E.phase = ph.name
            run(ph)

    phases(FIRST)
    with E.segment("mlp", 4):
        phases(MLP)
    with E.segment("layer", 2):
        phases(LAYER)


def group_loop(E, count, parity):
    yield 0, parity, True
    turns = (count - 1) // 2
    if turns >= 2:
        with E.loop(turns) as it:
            for u in (0, 1):
                yield it * 2 + (1 + u), (parity + 1 + u) % 2, False
    else:
        for g in range(1, 1 + 2 * turns):
            yield g, (parity + g) % 2, False
    if (count - 1) % 2:
        yield count - 1, (parity + count - 1) % 2, False


def chunk_loop(E):
    yield 0, True
    with E.loop(KC - 1) as it:
        yield it + 1, False


def groups_of(E, ph):
    done = 0
    for r, (count, _) in enumerate(ph.groups):
        for g, par, first in group_loop(E, count, (START[ph.name].get("group", 0) + done) % 2):
            yield g + done, g, r, par, first and done == 0
        done += count


def row(t, i):
    return t[:, bass.ds(i, 1), :].rearrange("p a s -> p (a s)")


def units_of(kind):
    def of(half, i):
        if kind == "att_c":
            return [(half, i, "win", 0, i + 1), (half, i, "sel", 0, i + 1), (half, i, "cmp", 0, 0)]
        lo = max(0, i - 1) if kind == "att_b" else 0
        return [(half, i, "one", lo, i + 1 - lo)]

    small_first, large_first = (0, 3, 1, 2), (3, 0, 2, 1)
    one = [u for i in small_first for u in of(0, i)]
    if kind == "att_a":
        order = [u for i in small_first for half in (0, 1) for u in of(half, i)]
    else:
        order = [u for two in zip(one, [u for i in large_first for u in of(1, i)]) for u in two]
    out = []
    for pair, units in enumerate((order, order[::-1])):
        same = [(u[1], kind != "att_a" and u[0]) for u in units]
        out += [(pair, *u, same.index(w) == j, w not in same[j + 1:])
                for j, (u, w) in enumerate(zip(units, same))]
    return out


def build(nc, x_in, w_first, w_mlp, w_layer, ada, first_small, layer_small, biases, cmp_w1, lam_in, c_in,
          consts, out):
    ctx = ExitStack()
    with ctx:
        def sb(name, shape, dt=F32):
            return ctx.enter_context(nc.sbuf_tensor(name, shape, dt))

        x = sb("x", [P, KC, S])
        h_hi = sb("h_hi", [P, KC, S], F32R)
        h_lo = sb("h_lo", [P, KC, S], F32R)
        raw = sb("raw", [P, 2, RAW])
        w_hi = sb("w_hi", [P, PIECES, SLOT], F32R)
        w_lo = sb("w_lo", [P, PIECES, SLOT], F32R)
        small = sb("small", [P, SM_N])
        lay = sb("lay", [P, LY_N])
        cst = sb("cst", [P, CS_N])
        ones = sb("ones", [P, P])
        mods = sb("mods", [P, 2 * 3 * KC])
        mod = sb("mod", [P, MODS])
        mod_part = sb("mod_part", [P, ADA])
        norm_a = sb("norm_a", [P, KC])
        norm_b = sb("norm_b", [P, KC])
        res_scale = sb("res_scale", [P, KC])
        gates = sb("gates", [P, TB, GATES])
        kc_sb = sb("kc_sb", [P, CMP_N])
        vc_sb = sb("vc_sb", [CMP_N, P])
        row_max = sb("row_max", [P, 4])
        neg_max = sb("neg_max", [P, 4])
        row_sum = sb("row_sum", [P, 4])
        row_inv = sb("row_inv", [P, 4])
        row_scale = sb("row_scale", [P, 4])
        neg_lam = sb("neg_lam", [P, 1])
        lam_t = sb("lam_t", [P, 4])
        tiny_t = sb("tiny_t", [P, 1])
        ident_16 = sb("ident_16", [P, P], mybir.dt.bfloat16)
        tri_16 = sb("tri_16", [P, P], mybir.dt.bfloat16)
        eps_t = sb("eps_t", [P, len(ROOTS)])

        arena_kb = 83
        arena = sb("arena", [P, int(arena_kb * 256)])
        first_byte = nc.sbuf_base - int(arena_kb * 1024)

        def at(name, kb, shape, dt=F32):
            assert kb * 1024 + int(np.prod(shape[1:])) * 4 <= arena_kb * 1024, name
            return nc.alloc_sbuf_tensor_at(name, shape, dt, offset=first_byte + int(kb * 1024))

        qk = at("qk", 0, [P, 9, S])
        v_all = at("v_all", 18, [P, TB, S])
        v_bc = at("v_bc", 18, [P, TB, V_BC])
        branch = at("branch", 26, [P, 3 * 4, S])
        q_st = at("q_st", 50, [P, 2, S])
        k_st = at("k_st", 54, [P, 2, S])
        v_st = at("v_st", 58, [P, 2, TB, P])
        s_sb = at("s_sb", 62, [P, 4, S + 8])
        pt_sb = at("pt_sb", 70.25, [P, 2, S])
        bias_t = at("bias_t", 74.25, [P, 2, 2, S])
        c_t = at("c_t", 50, [P, D])
        lam_w = at("lam_w", 54, [P, 4, HALF])
        sq_t = at("sq_t", 62, [P, 2, S])
        inv_t = at("inv_t", 66, [P, 2, S])
        rs_t = at("rs_t", 70, [P, 2, S])
        cmp_w = at("cmp_w", 50, [P, CMP_STRIDE, 2 * P])
        cmp_t = at("cmp_t", 66, [P, 2, S])
        cmp_x = at("cmp_x", 70, [P, CMP_STRIDE, 2, CMP_N])
        cmp_h = at("cmp_h", 82.25, [P, 2, 2 * CMP_N])
        cmp_s = at("cmp_s", 82.75, [P, 2, CMP_N])
        pool_s = at("pool_s", 50, [P, 2, S])
        pool_d = at("pool_d", 54, [P, S])
        f_t = at("f_t", 56, [8, 5, S])
        br_hi = at("br_hi", 0, [P, 12, S], F32R)
        br_lo = at("br_lo", 50, [P, 12, S], F32R)
        merged = at("merged", 26, [P, KC, S])
        sig_t = at("sig_t", 42, [P, 3, S])
        prod_t = at("prod_t", 48, [P, S])
        nsq = at("nsq", 60, [P, 2, S])
        nroot = at("nroot", 64, [P, S])
        a_hi = at("a_hi", 0, [P, KC, S], F32R)
        a_lo = at("a_lo", 16, [P, KC, S], F32R)
        g_sb = at("g_sb", 32, [P, 2, S])
        ada_t = at("ada_t", 36, [P, 2, ADA, D])
        ada_junk = at("ada_junk", 66, [P, D])

        S_BANKS = (0, 1, 6, 7)
        V_BANKS = (6, 7, 0, 1)
        psum = ctx.enter_context(nc.psum_tensor("psum", [P, 8 * S], F32))

        def root_of(what):
            n = list(ROOTS).index(what)
            return dict(scale=ROOTS[what][0], bias=eps_t[:, n:n + 1])

        def bank(b, n=S):
            return psum[:, b * S:b * S + n]

        c_bcast = psum[:, 6 * S:8 * S]
        nrs = bank(5)
        nt = [bank(2), bank(3)]
        cum_dram = nc.dram_tensor("cum_dram", (8, S), F32).ap()

        sem = {n: ctx.enter_context(nc.semaphore(n)) for n in SEMS}
        raw_loaded, bias_loaded, ada_loaded = [ctx.enter_context(nc.semaphore(f"raw_loaded{i}")) for i in (0, 1)], \
            (sem["bias0"], sem["bias1"]), (sem["ada0"], sem["ada1"])
        act_chain, dve_chain, pool_chain = (ctx.enter_context(nc.semaphore(f"{n}_chain"))
                                            for n in ("act", "dve", "pool"))
        out_done = ctx.enter_context(nc.semaphore("out_done"))
        ident = cst[:, CS["ident"]:CS["ident"] + P]
        pair_ones = cst[:, CS["pair_ones"]:CS["pair_ones"] + P]
        block = ctx.enter_context(nc.Block())

        @block.sync
        def _(sp):
            E = Engine(sp, "sp")
            offset = {"first": 0, "mlp": 0, "layer": 0}

            sp.dma_start(small[:], first_small).then_inc(sem["prep_loaded"], 16)
            sp.dma_start(cst[:], consts).then_inc(sem["prep_loaded"], 16)
            sp.dma_start(lam_w[:], lam_in).then_inc(sem["prep_loaded"], 16)
            sp.dma_start(x[:, 0:4, :], x_in[:, 0:4, :]).then_inc(sem["prep_loaded"], 16)
            sp.dma_start(x[:, 4:8, :], x_in[:, 4:8, :]).then_inc(sem["prep_loaded"], 16)

            def bias_tiles(kind):
                tile0 = dict(att_a=0, att_b=4, att_c=12, att_a2=20, att_c2=0)[kind]
                if kind == "att_c2":
                    sp.wait_ge(sem["cum_stored"], E.at("cum_stored", 0))
                with E.loop(2) as it:
                    for u in (0, 1):
                        sp.wait_ge(sem["pair_done"], E.at("pair_done", it * 2 + u - 1))
                        for t in range(TILES[kind]):
                            if kind == "att_c2":
                                src = cum_dram[bass.ds((it * 2 + u) * 2 + t, 1), :].to_broadcast([P, S])
                            else:
                                tile = (it * 2 + u) * TILES[kind] + (t + tile0)
                                if kind == "att_a2":
                                    tile = E.turn * 8 + tile
                                src = biases[bass.ds(tile, 1), :, :].rearrange("a p s -> p (a s)")
                            sp.dma_start(bias_t[:, u, t, :], src).then_inc(bias_loaded[u], 16)

            def run(ph):
                src = {"first": w_first, "mlp": w_mlp, "layer": w_layer}[E.seg]
                for gi, g, r, par, first in groups_of(E, ph):
                    size = ph.groups[r][1]
                    n = PIECES * size
                    at_run = offset[E.seg] + sum(c * PIECES * f * P for c, f in ph.groups[:r])
                    start = g * (n * P) + at_run
                    if E.turn is not None:
                        start = E.turn * sum(q.floats for q in dict(mlp=MLP, layer=LAYER)[E.seg]) + start
                    sp.wait_ge(sem["w_lo"], E.at("w_lo", gi * PIECES - PIECES))
                    sp.dma_start(raw[:, par, 0:n],
                                 src[bass.ds(start, n * P)].rearrange("(p n) -> p n", p=P))\
                        .then_inc(raw_loaded[par], 16)
                offset[E.seg] += ph.floats
                if ph.kind.startswith("att"):
                    bias_tiles(ph.kind)

            walk(E, run)
            sp.wait_ge(sem["phase_done"], sum(ph.totals["phase_done"] * n for _, phases, n in SEGMENTS for ph in phases))
            sp.dma_start(out, x[:]).then_inc(out_done, 16)
            sp.wait_ge(out_done, 16)

        @block.gpsimd
        def _(pool):
            E = Engine(pool, "pool")
            nc.gpsimd.memset(ones[:], 1.0).then_inc(pool_chain, 1)
            pool.wait_ge(pool_chain, E.step())
            for n, (_, eps) in enumerate(ROOTS.values()):
                nc.gpsimd.memset(eps_t[:, n:n + 1], eps).then_inc(pool_chain, 1)
                pool.wait_ge(pool_chain, E.step())
            pool.nop().then_inc(sem["prep_step"], 1)
            pool.nop().then_inc(sem["w_lo"], PRESET["w_lo"])
            pool.nop().then_inc(sem["pair_done"], 2)

            def raw_count(ph, gi, par):
                before = gi + START[ph.name].get("group", 0)
                if E.turn is not None:
                    before = E.turn * PER[E.seg]["group"] + before
                return before

            def split(ph):
                for gi, g, r, par, first in groups_of(E, ph):
                    size = ph.groups[r][1]
                    pool.wait_ge(raw_loaded[par], raw_count(ph, gi, par) * 8 + (16 if par == 0 else 8))
                    for k in range(PIECES):
                        piece = raw[:, par, k * size:(k + 1) * size]
                        pool.wait_ge(sem["w_used"], E.at("w_used", gi * PIECES + k + 1 - PIECES))
                        nc.gpsimd.tensor_tensor(w_hi[:, k, 0:size], piece, ones[:, 0:1].to_broadcast([P, size]),
                                                ALU.mult)\
                            .then_inc(sem["w_hi"], 1)
                        pool.wait_ge(sem["w_hi"], E.at("w_hi", gi * PIECES + k + 1))
                        nc.gpsimd.tensor_tensor(w_lo[:, k, 0:size], piece, w_hi[:, k, 0:size].bitcast(F32),
                                                ALU.subtract).then_inc(sem["w_lo"], 1)

            def stage(ph):
                kind = ph.kind
                keys_too = kind in ("att_a", "att_a2", "att_c2")
                if kind == "att_c":
                    pool.wait_ge(sem["phase_done"], E.at("phase_done", 0))
                pool.wait_ge(sem["qk_out"], E.at("qk_out", 0))
                masks = {"att_b": ((2 * P, "window"), (3 * P, "tri")), "att_a2": ((3 * P, "chunk"),),
                         "att_c2": ()}.get(kind, ((3 * P, "tri"),))
                with E.loop(2) as it:
                    for u in (0, 1):
                        pool.wait_ge(sem["pair_done"], E.at("pair_done", it * 2 + u - 1))
                        pool.nop(nofuse=True)
                        if keys_too:
                            nc.gpsimd.tensor_copy(k_st[:, u, :], row(qk, it * 2 + (4 + u))).then_inc(pool_chain, 1)
                            pool.wait_ge(pool_chain, E.step())
                            pool.nop(nofuse=True)
                        nc.gpsimd.tensor_copy(q_st[:, u, :], row(qk, it * 2 + u)).then_inc(sem["staged"], 1)
                        if masks:
                            pool.wait_ge(bias_loaded[u], E.at(f"bias{u}", (it + 1) * (16 * TILES[kind])))
                            pool.nop(nofuse=True)
                        for t in range(TILES[kind]):
                            for m, (at_col, mask) in enumerate(masks):
                                tile = bias_t[:, u, t, at_col:at_col + P]
                                last = t == TILES[kind] - 1 and m == len(masks) - 1
                                done = sem["bias_masked"] if last else pool_chain
                                nc.gpsimd.tensor_tensor(tile, tile, cst[:, CS[mask]:CS[mask] + P], ALU.add)\
                                    .then_inc(done, 1)
                                if not last:
                                    pool.wait_ge(pool_chain, E.step())
                        if keys_too:
                            pool.wait_ge(sem["plain_out"], E.at("plain_out", 0))
                            pool.nop(nofuse=True)
                            nc.gpsimd.tensor_copy(v_st[:, u, :, :],
                                                  v_all[:, :, bass.ds(it * (2 * P) + u * P, P)])\
                                .then_inc(sem["v_staged"], 1)

            def run(ph):
                if ph.groups:
                    split(ph)
                if ph.kind.startswith("att"):
                    stage(ph)

            walk(E, run)

        @block.tensor
        def _(pe):
            E = Engine(pe, "pe")
            mm = nc.tensor.matmul
            pe.nop().then_inc(sem["w_used"], PRESET["w_used"])

            def mm3(dst, lh, ll, rh, rl, first, last):
                mm(dst, lh, rh, start=first, stop=False)
                mm(dst, lh, rl, start=False, stop=False)
                return mm(dst, ll, rh, start=False, stop=last)

            def piece_ready(ph, gi, k):
                pe.wait_ge(sem["w_lo"], E.at("w_lo", gi * PIECES + k + 1))

            def tiles(dst, k, t0, n, hi, lo, c0, first, last, fresh=False):
                for t in range(n):
                    if fresh:
                        pe.wait_ge(sem["h_lo"], E.at("h_lo", c0 + t + 1 - KC))
                    w = slice((t0 + t) * P, (t0 + t + 1) * P)
                    ins = mm3(dst, w_hi[:, k, w], w_lo[:, k, w], hi[:, c0 + t, :], lo[:, c0 + t, :],
                              first and t == 0, last and t == n - 1)
                return ins

            def norm_sum(c):
                pe.wait_ge(sem["norm_squared"], E.at("norm_squared", c + 1))
                mm(bank(4), ones[:], nsq[:, c % 2, :], start=c == 0, stop=c == KC - 1)\
                    .then_inc(sem["norm_summed"], 1)

            def norm(ph):
                if ph.name not in SUMMED_BEFORE:
                    for c in range(KC):
                        norm_sum(c)

            def qk_sum(ph, j, n):
                pe.wait_ge(sem["qk_squared"], E.at("qk_squared", j + 1))
                if j >= 2:
                    pe.wait_ge(sem["qk_rstd"], E.at("qk_rstd", j - 1))
                mm(bank(4 + j % 2, n), pair_ones, sq_t[:, j % 2, 0:n], start=True, stop=True)\
                    .then_inc(sem["qk_summed"], 1)

            def full_group(ph, gi, free, fresh=False):
                for k in range(PIECES):
                    piece_ready(ph, gi, k)
                    if free:
                        free(k)
                    tiles(bank(k), k, 0, KC, h_hi, h_lo, 0, True, True, fresh and k == 0)\
                        .then_inc(sem["w_used"], 1)
                    yield k

            def thin_group(ph, gi, b, free):
                for k in range(PIECES):
                    piece_ready(ph, gi, k)
                    if k == 0 and free:
                        free()
                    tiles(bank(b), k, 0, 2, h_hi, h_lo, 2 * k, k == 0, k == PIECES - 1)\
                        .then_inc(sem["w_used"], 1)

            def token_group(ph, gi, cols, banks, free):
                for k in range(PIECES):
                    piece_ready(ph, gi, k)
                    for t in range(2):
                        c = 2 * k + t
                        w = slice(t * cols, (t + 1) * cols)
                        for b in range(TB):
                            if c == 0 and free:
                                free(b)
                            tok = slice(b * P, (b + 1) * P)
                            ins = mm3(bank(banks[b], cols), h_hi[:, c, tok], h_lo[:, c, tok], w_hi[:, k, w],
                                      w_lo[:, k, w], c == 0, c == KC - 1)
                    ins.then_inc(sem["w_used"], 1)

            def proj(ph):
                kind = ph.kind
                if kind in ("proj_a", "proj_a2", "proj_c2"):
                    for g in range(2):
                        free = (lambda k: pe.wait_ge(sem["qk_out"], E.at("qk_out", k + 1))) if g else None
                        for k in full_group(ph, g, free, kind != "proj_c2" and g == 0):
                            if k:
                                qk_sum(ph, 4 * g + k - 1, S)
                        qk_sum(ph, 4 * g + 3, S)
                    def free(b):
                        if b >= 2:
                            pe.wait_ge(sem["qk_out"], E.at("qk_out", 4 + b - 1))
                    token_group(ph, 2, S, V_BANKS, free)
                elif kind == "proj_bc":
                    for k in full_group(ph, 0, None):
                        if k:
                            qk_sum(ph, k - 1, S)
                    qk_sum(ph, 3, S)
                    for k in full_group(ph, 1, lambda k: pe.wait_ge(sem["qk_out"], E.at("qk_out", k + 1))):
                        if k:
                            qk_sum(ph, 4 + k - 1, S)
                    thin_group(ph, 2, 0, lambda: pe.wait_ge(sem["qk_out"], E.at("qk_out", 5)))
                    def free(b):
                        if b == 0:
                            pe.wait_ge(sem["plain_out"], E.at("plain_out", 2))
                        elif b == 3:
                            pe.wait_ge(sem["plain_out"], E.at("plain_out", 1))
                        else:
                            pe.wait_ge(sem["qk_out"], E.at("qk_out", 5 + b))
                    token_group(ph, 3, V_BC, range(TB), free)
                elif kind == "proj_cq":
                    for k in full_group(ph, 0, None):
                        if k:
                            qk_sum(ph, k - 1, S)
                    qk_sum(ph, 3, S)
                elif kind == "proj_u":
                    for k in full_group(ph, 0, None):
                        pass
                    thin_group(ph, 1, 4, None)

            def attention(ph):
                kind = ph.kind
                units = units_of(kind)
                n = len(units) // 2
                with E.loop(2) as it:
                    def score(j):
                        u, half, i, br, lo, blocks, start, stop = units[j]
                        rows = slice(half * HALF, (half + 1) * HALF)
                        if j % n == 0:
                            pe.wait_ge(sem["staged"], E.at("staged", it * 2 + u + 1))
                        q = q_st[rows, u, i * P:(i + 1) * P]
                        b = bank(S_BANKS[j % 4])
                        pe.nop(nofuse=True)
                        if br == "cmp":
                            mm(b[:, 0:CMP_N], q, kc_sb[rows, :], start=True, stop=True)\
                                .then_inc(sem["scores"], 1)
                            return
                        cols = slice(lo * P, (lo + blocks) * P)
                        k = {"att_b": qk[rows, 4, cols], "att_c": qk[rows, 5 if br == "sel" else 6, cols]}\
                            .get(kind, k_st[rows, u, cols])
                        w = blocks * P
                        if kind == "att_c2":
                            mm(b[:, 0:w], q, k, start=True, stop=False)
                            mm(b[:, w - P:w], ident_16[:], tri_16[:], start=False, stop=True)\
                                .then_inc(sem["scores"], 1)
                        else:
                            mm(b[:, 0:w], q, k, start=True, stop=True).then_inc(sem["scores"], 1)

                    def transposes(j):
                        u, half, i, br, lo, blocks, start, stop = units[j]
                        pe.wait_ge(sem["probs"], E.at("probs", it * (2 * n) + j + 1))
                        t_bank = bank(2 + j % 2)
                        pe.nop(nofuse=True)
                        if br == "cmp":
                            nc.tensor.transpose(t_bank[0:CMP_N, 0:P], s_sb[:, j % 4, 0:CMP_N], ident)\
                                .then_inc(sem["transposed"], 1)
                        else:
                            for b in range(blocks):
                                ins = nc.tensor.transpose(t_bank[:, b * P:(b + 1) * P],
                                                          s_sb[:, j % 4, b * P:(b + 1) * P], ident)
                            ins.then_inc(sem["transposed"], 1)

                    for j in range(DEPTH):
                        score(j)
                    transposes(0)
                    for j in range(2 * n):
                        if j + DEPTH < 2 * n:
                            score(j + DEPTH)
                        if j + 1 < 2 * n:
                            transposes(j + 1)
                        u, half, i, br, lo, blocks, start, stop = units[j]
                        if j % n == 0 and kind not in ("att_b", "att_c"):
                            pe.wait_ge(sem["v_staged"], E.at("v_staged", it * 2 + u + 1))
                        pe.wait_ge(sem["pt_copied"], E.at("pt_copied", it * (2 * n) + j + 1))
                        pe.nop(nofuse=True)
                        wide = kind == "att_a"
                        o = psum[slice(0, P) if wide else slice(half * HALF, (half + 1) * HALF),
                                 (4 + u) * S + i * P:(4 + u) * S + (i + 1) * P]
                        if br == "cmp":
                            ins = mm(o, vc_sb[:, half * HALF:(half + 1) * HALF], pt_sb[0:CMP_N, j % 2, 0:P],
                                     start=start, stop=stop)
                        else:
                            for b in range(blocks):
                                if kind == "att_b":
                                    v = v_bc[:, lo + b, half * HALF:(half + 1) * HALF]
                                elif kind == "att_c":
                                    c = (P if br == "sel" else 2 * P) + half * HALF
                                    v = v_bc[:, lo + b, c:c + HALF]
                                elif wide:
                                    v = v_st[:, u, b, :]
                                else:
                                    v = v_st[:, u, b, half * HALF:(half + 1) * HALF]
                                ins = mm(o, v, pt_sb[:, j % 2, b * P:(b + 1) * P],
                                         start=start and b == 0, stop=stop and b == blocks - 1)
                        ins.then_inc(sem["pv"], 1)

            def compress(ph):
                for kv in (0, 1):
                    pe.wait_ge(sem["cmp_loaded"], E.at("cmp_loaded", 16 * (kv + 1)))
                    pe.wait_ge(sem["cmp_dve"], E.at("cmp_dve", 3 * kv + 1))
                    for hid in (0, 1):
                        for j in range(CMP_STRIDE):
                            ins = mm(bank(hid, 2 * CMP_N), cmp_w[:, j, hid * P:(hid + 1) * P],
                                     cmp_x[:, j, :, :].rearrange("p g c -> p (g c)"),
                                     start=j == 0, stop=j == CMP_STRIDE - 1)
                    ins.then_inc(sem["cmp_pe"], 1)
                    pe.wait_ge(sem["cmp_act"], E.at("cmp_act", 3 * kv + 1))
                    pe.nop(nofuse=True)
                    for g in (0, 1):
                        for hid in (0, 1):
                            w2 = small[:, SM["w2"] + (2 * kv + hid) * HALF:SM["w2"] + (2 * kv + hid + 1) * HALF]
                            hx = cmp_h[:, hid, g * CMP_N:(g + 1) * CMP_N]
                            if kv == 0:
                                ins = mm(psum[g * HALF:(g + 1) * HALF, 2 * S:2 * S + CMP_N], w2, hx,
                                         start=hid == 0, stop=hid == 1)
                            else:
                                ins = mm(psum[0:CMP_N, 2 * S + g * HALF:2 * S + (g + 1) * HALF], hx, w2,
                                         start=hid == 0, stop=hid == 1)
                    ins.then_inc(sem["cmp_pe"], 1)
                    if kv == 0:
                        pe.wait_ge(sem["cmp_act"], E.at("cmp_act", 2))
                        mm(bank(3, CMP_N), pair_ones, cmp_s[:, 0, :], start=True, stop=True)\
                            .then_inc(sem["cmp_pe"], 1)

            def merge(ph):
                per = MIX_TILES // PIECES
                for d, first in chunk_loop(E):
                    for n in range(3):
                        for k in range(PIECES):
                            piece_ready(ph, 3 * d + n, k)
                            for t in range(k * per, (k + 1) * per):
                                gate = t < KC
                                if not first and t == 0:
                                    pe.wait_ge(sem["gate_sig"], E.at("gate_sig", d * 3 + n - 2))
                                if not first and t == KC:
                                    pe.wait_ge(sem["y_read"], E.at("y_read", d * 3 + n - 2))
                                if first and not gate:
                                    pe.wait_ge(sem["br_lo"], E.at("br_lo", 4 * n + t - KC + 1 - 12))
                                if first and n == 2 and t == 0:
                                    pe.wait_ge(sem["qk_rstd"], E.at("qk_rstd", 0))
                                w = slice((t - k * per) * P, (t - k * per + 1) * P)
                                c = t if gate else 4 * n + t - KC
                                hi, lo = (h_hi, h_lo) if gate else (br_hi, br_lo)
                                ins = mm3(bank(2 * n + (not gate)), w_hi[:, k, w], w_lo[:, k, w], hi[:, c, :],
                                          lo[:, c, :], t in (0, KC), t in (KC - 1, MIX_TILES - 1))
                            ins.then_inc(sem["w_used"], 1)

            def split_a(ph):
                for j in range(4):
                    pe.wait_ge(sem["qk_squared"], E.at("qk_squared", j + 1))
                    if j >= 2:
                        pe.wait_ge(sem["qk_rstd"], E.at("qk_rstd", j - 1))
                    mm(bank(4 + j % 2), ones[:], sq_t[:, j % 2, :], start=True, stop=True)\
                        .then_inc(sem["qk_summed"], 1)

            def up(ph):
                ffn = ph.kind == "ffn_up"
                for gi, g, r, par, first in groups_of(E, ph):
                    for k in range(PIECES):
                        piece_ready(ph, gi, k)
                        if not first:
                            if ffn and k % 2:
                                pe.wait_ge(sem["product"], E.at("product", g * 2 + (k // 2 - 1)))
                            elif ffn:
                                pe.wait_ge(sem["gated"], E.at("gated", g * 2 + (k // 2 - 1)))
                            else:
                                pe.wait_ge(sem["product"], E.at("product", g * 4 + (k - 3)))
                        tiles(bank(k), k, 0, KC, h_hi, h_lo, 0, True, True,
                              first and k == 0 and ph.name in ("mlp_up", "upa0", "upb0"))\
                            .then_inc(sem["w_used"], 1)

            def down(ph):
                n = ph.groups[0][1] // P
                hi, lo = (h_hi, h_lo) if ph.name.startswith("wout") else (a_hi, a_lo)
                for gi, g, r, par, first in groups_of(E, ph):
                    for k in range(PIECES):
                        piece_ready(ph, gi, k)
                        if not first:
                            pe.wait_ge(sem["x_added"], E.at("x_added", g * 4 + (k - 3)))
                        tiles(bank(k), k, 0, n, hi, lo, 0, True, True,
                              first and k == 0 and ph.name.startswith("wout")).then_inc(sem["w_used"], 1)
                        if ph.name in SUMMING and g * 4 + k >= 2:
                            norm_sum(g * 4 + k - 2)
                if ph.name in SUMMING:
                    norm_sum(KC - 2)
                    norm_sum(KC - 1)

            def pool_mix(ph):
                for g in range(4):
                    pe.wait_ge(sem["pool_in"], E.at("pool_in", g + 1))
                    if g >= 2:
                        pe.wait_ge(sem["pool_out"], E.at("pool_out", g - 1))
                    w = lay[:, LY["pool"] + g * P:LY["pool"] + (g + 1) * P]
                    mm(bank(g % 2), w, pool_d[:], start=True, stop=True).then_inc(sem["pool_mm"], 1)

            def run(ph):
                kind = ph.kind
                if kind == "prep":
                    pe.wait_ge(sem["prep_step"], E.at("prep_step", 4))
                elif kind == "norm":
                    norm(ph)
                elif kind.startswith("proj"):
                    proj(ph)
                elif kind.startswith("att"):
                    attention(ph)
                elif kind == "compress":
                    compress(ph)
                elif kind == "split1":
                    split_a(ph)
                elif kind == "merge":
                    merge(ph)
                elif kind.endswith("up"):
                    up(ph)
                elif kind == "down":
                    down(ph)
                elif kind == "pool":
                    pool_mix(ph)
                if not ph.meets:
                    return
                pe.nop(nofuse=True)
                pe.drain().then_inc(sem["phase_done"], 1)
                pe.wait_ge(sem["phase_done"], E.at("phase_done", 3))

            walk(E, run)

        @block.scalar
        def _(act):
            E = Engine(act, "act")
            fn = nc.scalar.activation

            def norm_square(c):
                if c >= 2:
                    act.wait_ge(sem["norm_summed"], E.at("norm_summed", c - 1))
                fn(nsq[:, c % 2, :], x[:, c, :], ACT.Square).then_inc(sem["norm_squared"], 1)

            def norm(ph):
                summed = ph.name in SUMMED_BEFORE
                if not summed:
                    for c in range(KC):
                        norm_square(c)
                act.wait_ge(sem["norm_summed"], E.at("norm_summed", 0 if summed else KC))
                fn(nroot[:], bank(4), ACT.Sqrt, **root_of("model")).then_inc(sem["norm_root"], 1)
                for c in range(KC):
                    act.wait_ge(sem["norm_scaled"], E.at("norm_scaled", c + 1))
                    fn(h_hi[:, c, :], nt[c % 2], ACT.Identity, bias=norm_b[:, c:c + 1])\
                        .then_inc(sem["h_hi"], 1)

            def square(ph, j, src, n=S):
                if j >= 2:
                    act.wait_ge(sem["qk_summed"], E.at("qk_summed", j - 1))
                fn(sq_t[:, j % 2, 0:n], src, ACT.Square).then_inc(sem["qk_squared"], 1)

            def root(ph, j):
                what = "differential" if ph.kind == "split1" else "query" if j < 4 else "key"
                act.wait_ge(sem["qk_summed"], E.at("qk_summed", j + 1))
                if j >= 2:
                    act.wait_ge(sem["qk_inverse"], E.at("qk_inverse", j - 1))
                fn(rs_t[:, j % 2, :], bank(4 + j % 2), ACT.Sqrt, **root_of(what)).then_inc(sem["qk_rstd"], 1)

            def normed_blocks(ph, gi, j0, n):
                for k in range(n):
                    act.wait_ge(sem["w_used"], E.at("w_used", gi * PIECES + k + 1))
                    square(ph, j0 + k, bank(k))
                    if k:
                        root(ph, j0 + k - 1)
                root(ph, j0 + n - 1)

            def proj(ph):
                kind = ph.kind
                if kind in ("proj_a", "proj_a2", "proj_c2"):
                    normed_blocks(ph, 0, 0, 4)
                    normed_blocks(ph, 1, 4, 4)
                    act.wait_ge(sem["w_used"], E.at("w_used", 12))
                    for b in range(TB):
                        fn(v_all[:, b, :], bank(V_BANKS[b]), ACT.Copy).then_inc(sem["plain_out"], 1)
                elif kind == "proj_bc":
                    normed_blocks(ph, 0, 0, 4)
                    normed_blocks(ph, 1, 4, 3)
                    act.wait_ge(sem["w_used"], E.at("w_used", 8))
                    fn(qk[:, 7, :], bank(3), ACT.Copy).then_inc(sem["plain_out"], 1)
                    act.wait_ge(sem["w_used"], E.at("w_used", 12))
                    fn(qk[:, 8, :], bank(0), ACT.Copy).then_inc(sem["plain_out"], 1)
                    act.wait_ge(sem["w_used"], E.at("w_used", 16))
                    for b in range(TB):
                        fn(v_bc[:, b, :], bank(b, V_BC), ACT.Copy).then_inc(sem["plain_out"], 1)
                    act.wait_ge(sem["plain_out"], E.at("plain_out", 6))
                    fn(gates[:], v_bc[:, :, V_BC - GATES:V_BC], ACT.Sigmoid)
                elif kind == "proj_cq":
                    normed_blocks(ph, 0, 0, 4)
                elif kind == "proj_u":
                    for k in range(PIECES):
                        act.wait_ge(sem["w_used"], E.at("w_used", k + 1))
                        fn(qk[:, k, :], bank(k), ACT.Copy).then_inc(sem["plain_out"], 1)
                    act.wait_ge(sem["w_used"], E.at("w_used", 8))
                    fn(f_t[:, 0, :], psum[0:8, 4 * S:5 * S], ACT.Copy).then_inc(sem["plain_out"], 1)

            def attention(ph):
                units = units_of(ph.kind)
                n = len(units) // 2
                extra = 1 if ph.kind == "att_b" else 0
                with E.loop(2) as it:
                    def exps(j):
                        u, half, i, br, lo, blocks, start, stop = units[j]
                        w = CMP_N if br == "cmp" else blocks * P + extra
                        act.wait_ge(sem["row_max"], E.at("row_max", it * (2 * n) + j + 1))
                        fn(s_sb[:, j % 4, 0:w], s_sb[:, j % 4, 0:w], ACT.Exp, bias=neg_max[:, j % 4:j % 4 + 1],
                           accum_out=row_sum[:, j % 4:j % 4 + 1]).then_inc(sem["exps"], 1)

                    for j in range(DEPTH):
                        exps(j)
                    for j in range(2 * n):
                        u, half, i, br, lo, blocks, start, stop = units[j]
                        act.wait_ge(sem["transposed"], E.at("transposed", it * (2 * n) + j + 1))
                        if br == "cmp":
                            fn(pt_sb[0:CMP_N, j % 2, 0:P], psum[0:CMP_N, (2 + j % 2) * S:(2 + j % 2) * S + P],
                               ACT.Copy).then_inc(sem["pt_copied"], 1)
                        else:
                            fn(pt_sb[:, j % 2, 0:blocks * P], bank(2 + j % 2, blocks * P), ACT.Copy)\
                                .then_inc(sem["pt_copied"], 1)
                        if j + DEPTH < 2 * n:
                            exps(j + DEPTH)

            def compress(ph):
                act.dma_start(cmp_w[:], cmp_w1[0]).then_inc(sem["cmp_loaded"], 16)
                for kv in (0, 1):
                    act.wait_ge(sem["cmp_pe"], E.at("cmp_pe", 3 * kv + 1))
                    for hid in (0, 1):
                        ins = fn(cmp_h[:, hid, :], bank(hid, 2 * CMP_N), ACT.Gelu_apprx_tanh)
                    ins.then_inc(sem["cmp_act"], 1)
                    if kv == 0:
                        act.dma_start(cmp_w[:], cmp_w1[1]).then_inc(sem["cmp_loaded"], 16)
                        act.wait_ge(sem["cmp_pe"], E.at("cmp_pe", 2))
                        fn(cmp_s[:, 0, :], bank(2, CMP_N), ACT.Square).then_inc(sem["cmp_act"], 1)
                        act.wait_ge(sem["cmp_dve"], E.at("cmp_dve", 2))
                        fn(cmp_s[:, 0, :], cmp_s[:, 1, :], ACT.Sqrt).then_inc(sem["cmp_act"], 1)
                act.wait_ge(sem["cmp_pe"], E.at("cmp_pe", 5))
                fn(vc_sb[:], psum[0:CMP_N, 2 * S:2 * S + P], ACT.Copy).then_inc(sem["cmp_act"], 1)

            def split(ph):
                if ph.kind == "split1":
                    for j in range(4):
                        square(ph, j, branch[:, j, :])
                        if j:
                            root(ph, j - 1)
                    root(ph, 3)
                    act.wait_ge(sem["qk_out"], E.at("qk_out", 4))
                for c in range(12):
                    fn(br_hi[:, c, :], branch[:, c, :], ACT.Copy).then_inc(sem["br_hi"], 1)

            def merge(ph):
                for d, first in chunk_loop(E):
                    for n in range(3):
                        act.wait_ge(sem["w_used"], E.at("w_used", (3 * d + n) * PIECES + (KC - 1) // 3 + 1))
                        if not first:
                            act.wait_ge(sem["y_read"], E.at("y_read", d * 3 + n - 2))
                        elif n == 0:
                            act.wait_ge(sem["br_lo"], E.at("br_lo", 0))
                        fn(sig_t[:, n, :], bank(2 * n), ACT.Sigmoid).then_inc(sem["gate_sig"], 1)

            def msplit(ph):
                for c in range(KC):
                    fn(h_hi[:, c, :], merged[:, c, :], ACT.Copy).then_inc(sem["h_hi"], 1)

            def ada_load(ph, gi):
                if ph.name not in ADA_LOADS or gi >= len(ADA_LOADS[ph.name]):
                    return
                n = ADA_LOADS[ph.name][gi]
                act.wait_ge(sem["ada_used"], E.at("ada_used", gi - 1))
                act.nop(nofuse=True)
                load = E.turn * 4 + n if E.seg == "mlp" else E.turn * 16 + (n + 16)
                act.dma_start(ada_t[:, n % 2, :, :], ada[bass.ds(load, 1), :, :].rearrange("a p n -> p (a n)"))\
                    .then_inc(ada_loaded[n % 2], 16)

            def up(ph):
                ffn = ph.kind == "ffn_up"
                per = 2 if ffn else 4
                func = ACT.Silu if ffn else ACT.Relu
                for gi, g, r, par, first in groups_of(E, ph):
                    def part(k):
                        act.wait_ge(sem["product"], E.at("product", g * per + k + 1))
                        act.nop(nofuse=True)
                        fn(row(a_hi, g * per + k), g_sb[:, k % 2, :], ACT.Copy)\
                            .then_inc(sem["act_hi"], 1)

                    for k in range(per):
                        if k == 0:
                            ada_load(ph, gi)
                        act.wait_ge(sem["w_used"], E.at("w_used", gi * PIECES + (2 * k if ffn else k) + 1))
                        if not first or k >= 2:
                            act.wait_ge(sem["act_lo"], E.at("act_lo", g * per + (k - 1)))
                        fn(g_sb[:, k % 2, :], bank(2 * k if ffn else k), func).then_inc(sem["gated"], 1)
                        if k:
                            part(k - 1)
                    part(per - 1)

            def down(ph):
                for gi, g, r, par, first in groups_of(E, ph):
                    ada_load(ph, gi)
                    if ph.name in SUMMING:
                        for k in range(PIECES):
                            act.wait_ge(sem["x_added"], E.at("x_added", g * 4 + k + 1))
                            norm_square(g * 4 + k)

            def pool_mix(ph):
                act.wait_ge(sem["forget_dve"], E.at("forget_dve", 1))
                fn(f_t[:, 2, :], f_t[:, 1, :], ACT.Abs).then_inc(act_chain, 1)
                act.wait_ge(act_chain, E.step())
                fn(f_t[:, 2, :], f_t[:, 2, :], ACT.Exp, scale=-1.0).then_inc(sem["forget_step"], 1)
                act.wait_ge(sem["forget_step"], E.at("forget_step", 1))
                fn(f_t[:, 3, :], f_t[:, 2, :], ACT.Ln, bias=1.0).then_inc(sem["forget_step"], 1)
                for g in range(4):
                    act.wait_ge(sem["pool_mm"], E.at("pool_mm", g + 1))
                    fn(branch[:, 4 + g, :], bank(g % 2), ACT.Copy,
                       scale=lay[:, LY["pool_scale"] + g:LY["pool_scale"] + g + 1]).then_inc(sem["pool_out"], 1)
                act.wait_ge(sem["forget_dve"], E.at("forget_dve", 3))
                act.dma_start(cum_dram, f_t[:, 4, :]).then_inc(sem["cum_stored"], 16)
                act.wait_ge(sem["cum_stored"], E.at("cum_stored", 16))

            def run(ph):
                kind = ph.kind
                if kind == "prep":
                    act.wait_ge(sem["prep_loaded"], E.at("prep_loaded", 80))
                    act.wait_ge(sem["prep_step"], E.at("prep_step", 3))
                    fn(lam_t[:, 2:4], lam_t[:, 0:2], ACT.Exp).then_inc(sem["prep_step"], 1)
                elif kind == "cond":
                    act.dma_start(c_t[:], c_in).then_inc(sem["layer_loaded"], 16)
                    act.wait_ge(sem["layer_loaded"], E.at("layer_loaded", 16))
                    fn(c_bcast, c_t[:], ACT.Silu)
                elif kind == "norm":
                    norm(ph)
                elif kind.startswith("proj"):
                    proj(ph)
                elif kind.startswith("att"):
                    attention(ph)
                elif kind == "compress":
                    compress(ph)
                elif kind.startswith("split"):
                    split(ph)
                elif kind == "merge":
                    merge(ph)
                elif kind == "msplit":
                    msplit(ph)
                elif kind.endswith("up"):
                    up(ph)
                elif kind == "down":
                    down(ph)
                elif kind == "pool":
                    pool_mix(ph)
                elif kind == "layer":
                    act.dma_start(c_t[:], c_in).then_inc(sem["layer_loaded"], 16)
                    act.dma_start(lay[:], layer_small[bass.ds(E.turn, 1), :, :].rearrange("a p n -> p (a n)"))\
                        .then_inc(sem["layer_loaded"], 16)
                    act.wait_ge(sem["layer_loaded"], E.at("layer_loaded", 32))
                    fn(c_bcast, c_t[:], ACT.Silu)
                if not ph.meets:
                    return
                act.nop(nofuse=True)
                act.drain().then_inc(sem["phase_done"], 1)
                act.wait_ge(sem["phase_done"], E.at("phase_done", 3))

            walk(E, run)

        @block.vector
        def _(dve):
            E = Engine(dve, "dve")
            v = nc.vector
            dve.nop().then_inc(sem["ada_used"], PRESET["ada_used"])

            def col(t, c, n=1):
                return t[:, c:c + n]

            def norm(ph):
                name = ph.name
                if name in ("norm_mix", "norm_mlp"):
                    v.tensor_copy(norm_a[:], col(small, SM["mix" if name == "norm_mix" else "mlp"], KC)).then_inc(dve_chain, 1)
                    dve.wait_ge(dve_chain, E.step())
                    v.memset(norm_b[:], 0.0).then_inc(dve_chain, 1)
                    dve.wait_ge(dve_chain, E.step())
                    v.memset(res_scale[:], 1.0).then_inc(dve_chain, 1)
                    dve.wait_ge(dve_chain, E.step())
                else:
                    n = {"norma": 0, "norm_l": 1, "normb": 2}[name]
                    v.tensor_scalar(norm_b[:], col(mod, (3 * n + 1) * KC, KC), 1.0, None, ALU.add).then_inc(dve_chain, 1)
                    dve.wait_ge(dve_chain, E.step())
                    v.tensor_tensor(norm_a[:], norm_b[:], col(lay, LY["gain"] + n * KC, KC), ALU.mult).then_inc(dve_chain, 1)
                    dve.wait_ge(dve_chain, E.step())
                    v.tensor_copy(norm_b[:], col(mod, 3 * n * KC, KC)).then_inc(dve_chain, 1)
                    dve.wait_ge(dve_chain, E.step())
                    v.tensor_scalar(res_scale[:], col(mod, (3 * n + 2) * KC, KC), 1.0 if n == 1 else 0.5,
                                    None, ALU.mult).then_inc(dve_chain, 1)
                    dve.wait_ge(dve_chain, E.step())
                dve.wait_ge(sem["norm_root"], E.at("norm_root", 1))
                v.reciprocal(nrs, nroot[:]).then_inc(dve_chain, 1)
                dve.wait_ge(dve_chain, E.step())

                def low(c):
                    dve.wait_ge(sem["h_hi"], E.at("h_hi", c + 1))
                    v.scalar_tensor_tensor(h_lo[:, c, :], nt[c % 2], norm_b[:, c:c + 1],
                                           h_hi[:, c, :].bitcast(F32), ALU.add, ALU.subtract)\
                        .then_inc(sem["h_lo"], 1)
                    dve.wait_ge(sem["h_lo"], E.at("h_lo", c + 1))

                for c in range(KC):
                    v.scalar_tensor_tensor(nt[c % 2], x[:, c, :], norm_a[:, c:c + 1], nrs,
                                           ALU.mult, ALU.mult).then_inc(sem["norm_scaled"], 1)
                    if c:
                        low(c - 1)
                low(KC - 1)

            def inverse(ph, j):
                dve.wait_ge(sem["qk_rstd"], E.at("qk_rstd", j + 1))
                if j >= 2:
                    dve.wait_ge(sem["qk_out"], E.at("qk_out", j - 1))
                v.reciprocal(inv_t[:, j % 2, :], rs_t[:, j % 2, :]).then_inc(sem["qk_inverse"], 1)

            def proj(ph):
                kind = ph.kind
                if kind == "proj_u":
                    return
                gain, where = dict(
                    proj_a=([(small, SM["gain"] + 0)] * 4 + [(small, SM["gain"] + 1)] * 4, range(8)),
                    proj_a2=([(lay, LY["qk"] + 0)] * 4 + [(lay, LY["qk"] + 1)] * 4, range(8)),
                    proj_c2=([(lay, LY["qk"] + 2)] * 4 + [(lay, LY["qk"] + 3)] * 4, range(8)),
                    proj_bc=([(small, SM["gain"] + 2)] * 4 + [(small, SM["gain"] + n) for n in (3, 6, 7)],
                             range(7)),
                    proj_cq=([(small, SM["gain"] + 4)] * 4, range(4)),
                )[kind]

                def finish(j):
                    t, c = gain[j]
                    dve.wait_ge(sem["qk_inverse"], E.at("qk_inverse", j + 1))
                    v.scalar_tensor_tensor(qk[:, where[j], :], bank(j % 4), t[:, c:c + 1], inv_t[:, j % 2, :],
                                           ALU.mult, ALU.mult).then_inc(sem["qk_out"], 1)

                for j in range(len(gain)):
                    inverse(ph, j)
                    if j:
                        finish(j - 1)
                finish(len(gain) - 1)

            def attention(ph):
                kind = ph.kind
                units = units_of(kind)
                n = len(units) // 2
                with E.loop(2) as it:
                    def maxima(j):
                        u, half, i, br, lo, blocks, start, stop = units[j]
                        pb = j % 4
                        if j % n == 0:
                            if kind == "att_c2":
                                dve.wait_ge(bias_loaded[u], E.at(f"bias{u}", (it + 1) * (16 * TILES[kind])))
                            else:
                                dve.wait_ge(sem["bias_masked"], E.at("bias_masked", it * 2 + u + 1))
                            dve.nop(nofuse=True)
                        if j >= 4:
                            dve.wait_ge(sem["transposed"], E.at("transposed", it * (2 * n) + (j - 3)))
                            dve.nop(nofuse=True)
                        first = -3e38
                        if kind == "att_b":
                            w = blocks * P
                            v.tensor_copy(s_sb[:, pb, w:w + 1],
                                          small[:, bass.ds(it * 4 + (SM["sinks"] + 2 * u + half), 1)]).then_inc(dve_chain, 1)
                            dve.wait_ge(dve_chain, E.step())
                            first = s_sb[:, pb, w:w + 1]
                        dve.wait_ge(sem["scores"], E.at("scores", it * (2 * n) + j + 1))
                        dve.nop(nofuse=True)
                        if br == "cmp":
                            c = CS["cmask"] + i * CMP_N
                            w, tile = CMP_N, cst[:, c:c + CMP_N]
                        else:
                            w = blocks * P
                            t = half if TILES[kind] == 2 else 0
                            c = 0 if kind == "att_c2" else (TB - 1 - i + lo) * P
                            tile = bias_t[:, u, t, c:c + w]
                        v.tensor_tensor_reduce(out=s_sb[:, pb, 0:w], in0=bank(S_BANKS[pb], w), in1=tile, scale=1.0,
                                               scalar=first, op0=ALU.add, op1=ALU.max,
                                               accum_out=row_max[:, pb:pb + 1]).then_inc(dve_chain, 1)
                        dve.wait_ge(dve_chain, E.step())
                        v.tensor_scalar(neg_max[:, pb:pb + 1], row_max[:, pb:pb + 1], -1.0, None, ALU.mult)\
                            .then_inc(sem["row_max"], 1)

                    def write_out(u):
                        dve.wait_ge(sem["pv"], E.at("pv", it * (2 * n) + (u + 1) * n))
                        dve.nop(nofuse=True)
                        b = dict(att_a=0, att_b=4, att_c=8, att_a2=0, att_c2=8)[kind]
                        v.tensor_copy(row(branch, it * 2 + (b + u)), bank(4 + u))\
                            .then_inc(sem["pair_done"], 1)

                    def normalise(j):
                        u, half, i, br, lo, blocks, start, stop = units[j]
                        pb = j % 4
                        w = CMP_N if br == "cmp" else blocks * P
                        dve.wait_ge(sem["exps"], E.at("exps", it * (2 * n) + j + 1))
                        v.reciprocal(row_inv[:, pb:pb + 1], row_sum[:, pb:pb + 1]).then_inc(dve_chain, 1)
                        dve.wait_ge(dve_chain, E.step())
                        factor = row_inv[:, pb:pb + 1]
                        if kind == "att_a" and half == 1:
                            v.tensor_tensor(row_scale[:, pb:pb + 1], factor, neg_lam[:], ALU.mult).then_inc(dve_chain, 1)
                            dve.wait_ge(dve_chain, E.step())
                            factor = row_scale[:, pb:pb + 1]
                        if kind == "att_c":
                            c = 3 * half + {"cmp": 0, "sel": 1, "win": 2}[br]
                            v.tensor_tensor(row_scale[:, pb:pb + 1], factor,
                                            gates[:, i, bass.ds(it * 12 + (6 * u + c), 1)], ALU.mult).then_inc(dve_chain, 1)
                            dve.wait_ge(dve_chain, E.step())
                            factor = row_scale[:, pb:pb + 1]
                            if br == "cmp" and i == 0:
                                v.tensor_tensor(factor, factor, cst[:, CS["valid"]:CS["valid"] + 1], ALU.mult).then_inc(dve_chain, 1)
                                dve.wait_ge(dve_chain, E.step())
                        v.tensor_scalar(s_sb[:, pb, 0:w], s_sb[:, pb, 0:w], factor, None, ALU.mult)\
                            .then_inc(sem["probs"], 1)

                    for j in range(DEPTH):
                        maxima(j)
                    normalise(0)
                    for j in range(2 * n):
                        if j + 1 < 2 * n:
                            normalise(j + 1)
                        if j + DEPTH < 2 * n:
                            maxima(j + DEPTH)
                        if j == n + 1:
                            write_out(0)
                    write_out(1)

            def compress(ph):
                for kv in (0, 1):
                    src = qk[:, 7 + kv, :]
                    if kv:
                        dve.wait_ge(sem["cmp_pe"], E.at("cmp_pe", 1))
                    for half in (0, 1):
                        for g in (0, 1):
                            v.tensor_copy(cmp_t[half * HALF:(half + 1) * HALF, g, 0:S - 1],
                                          src[g * HALF:(g + 1) * HALF, half:half + S - 1]).then_inc(dve_chain, 1)
                            dve.wait_ge(dve_chain, E.step())
                    pos = small[:, SM["pos"] + kv * CMP_STRIDE:SM["pos"] + (kv + 1) * CMP_STRIDE]
                    for g in (0, 1):
                        for part in (0, 1):
                            a = cmp_t[:, g, 16 * part:16 * part + CMP_N * 16]\
                                .rearrange("p (c j t) -> p j t c", j=8, t=2)[:, :, 0, :]
                            v.tensor_tensor(cmp_x[:, 8 * part:8 * part + 8, g, :], a,
                                            pos[:, 8 * part:8 * part + 8].unsqueeze(2).to_broadcast([P, 8, CMP_N]),
                                            ALU.add).then_inc(dve_chain, 1)
                            dve.wait_ge(dve_chain, E.step())
                    v.tensor_scalar(tiny_t[:], ones[:, 0:1], 1.0, None, ALU.mult).then_inc(sem["cmp_dve"], 1)
                    if kv == 0:
                        dve.wait_ge(sem["cmp_pe"], E.at("cmp_pe", 3))
                        v.tensor_scalar(cmp_s[:, 1, :], bank(3, CMP_N), 1.0 / HALF, EPS, ALU.mult, ALU.add).then_inc(dve_chain, 1)
                        dve.wait_ge(dve_chain, E.step())
                        v.reciprocal(cmp_s[:, 1, :], cmp_s[:, 1, :]).then_inc(sem["cmp_dve"], 1)
                        dve.wait_ge(sem["cmp_act"], E.at("cmp_act", 3))
                        v.scalar_tensor_tensor(kc_sb[:], bank(2, CMP_N), col(small, SM["gain"] + 5),
                                               cmp_s[:, 0, :], ALU.mult, ALU.mult).then_inc(sem["cmp_dve"], 1)

            def split(ph):
                if ph.kind == "split1":
                    def finish(j):
                        dve.wait_ge(sem["qk_inverse"], E.at("qk_inverse", j + 1))
                        v.scalar_tensor_tensor(branch[:, j, :], branch[:, j, :], col(small, SM["subln"]),
                                               inv_t[:, j % 2, :], ALU.mult, ALU.mult).then_inc(sem["qk_out"], 1)

                    for j in range(4):
                        inverse(ph, j)
                        if j:
                            finish(j - 1)
                    finish(3)
                    dve.wait_ge(sem["qk_out"], E.at("qk_out", 4))
                for c in range(12):
                    dve.wait_ge(sem["br_hi"], E.at("br_hi", c + 1))
                    v.tensor_tensor(br_lo[:, c, :], branch[:, c, :], br_hi[:, c, :].bitcast(F32), ALU.subtract)\
                        .then_inc(sem["br_lo"], 1)

            def merge(ph):
                dve.wait_ge(sem["br_lo"], E.at("br_lo", 0))
                for d, first in chunk_loop(E):
                    m = merged[:, 0, :] if first else row(merged, d)
                    for n in range(3):
                        dve.wait_ge(sem["gate_sig"], E.at("gate_sig", d * 3 + n + 1))
                        dve.wait_ge(sem["w_used"], E.at("w_used", (3 * d + n + 1) * PIECES))
                        v.tensor_tensor(prod_t[:] if n else m, sig_t[:, n, :], bank(2 * n + 1), ALU.mult)\
                            .then_inc(sem["y_read"], 1)
                        if n:
                            dve.wait_ge(sem["y_read"], E.at("y_read", d * 3 + n + 1))
                            v.tensor_tensor(m, m, prod_t[:], ALU.add).then_inc(dve_chain, 1)
                            dve.wait_ge(dve_chain, E.step())

            def msplit(ph):
                for c in range(KC):
                    dve.wait_ge(sem["h_hi"], E.at("h_hi", c + 1))
                    v.tensor_tensor(h_lo[:, c, :], merged[:, c, :], h_hi[:, c, :].bitcast(F32), ALU.subtract)\
                        .then_inc(sem["h_lo"], 1)

            def ada_sum(ph, gi):
                if ph.name not in ADA_LOADS or gi >= len(ADA_LOADS[ph.name]):
                    return
                n = ADA_LOADS[ph.name][gi]
                of_half = sum(m % 2 == n % 2 for m in ADA_LOADS[ph.name][:gi + 1])
                dve.wait_ge(ada_loaded[n % 2], E.at(f"ada{n % 2}", 16 * of_half))
                dve.nop(nofuse=True)
                for t in range(ADA):
                    ins = v.tensor_tensor_reduce(out=ada_junk[:], in0=ada_t[:, n % 2, t, :], in1=c_bcast, scale=1.0,
                                                 scalar=0.0, op0=ALU.mult, op1=ALU.add,
                                                 accum_out=mod_part[:, t:t + 1])
                    if t < ADA - 1:
                        ins.then_inc(dve_chain, 1)
                        dve.wait_ge(dve_chain, E.step())
                        dve.nop(nofuse=True)
                    else:
                        ins.then_inc(sem["ada_used"], 1)
                        dve.wait_ge(sem["ada_used"], E.at("ada_used", gi + 1))
                        dve.nop(nofuse=True)
                if E.seg == "mlp":
                    v.tensor_copy(mods[:, bass.ds(E.turn * 12 + 3 * n, ADA)], mod_part[:])\
                        .then_inc(dve_chain, 1)
                    dve.wait_ge(dve_chain, E.step())
                else:
                    c = 3 * KC + ADA * n
                    v.tensor_tensor(mod[:, c:c + ADA], mod_part[:], col(lay, LY["b_ada"] + c, ADA), ALU.add)\
                        .then_inc(dve_chain, 1)
                    dve.wait_ge(dve_chain, E.step())

            def up(ph):
                ffn = ph.kind == "ffn_up"
                per = 2 if ffn else 4
                for gi, g, r, par, first in groups_of(E, ph):
                    def low(k):
                        dve.wait_ge(sem["act_hi"], E.at("act_hi", g * per + k + 1))
                        v.tensor_tensor(row(a_lo, g * per + k), g_sb[:, k % 2, :],
                                        row(a_hi, g * per + k).bitcast(F32), ALU.subtract)\
                            .then_inc(sem["act_lo"], 1)

                    for k in range(per):
                        dve.wait_ge(sem["gated"], E.at("gated", g * per + k + 1))
                        dve.wait_ge(sem["w_used"], E.at("w_used", gi * PIECES + (2 * k + 1 if ffn else k) + 1))
                        v.tensor_tensor(g_sb[:, k % 2, :], g_sb[:, k % 2, :], bank(2 * k + 1 if ffn else k),
                                        ALU.mult).then_inc(sem["product"], 1)
                        if k == 0:
                            ada_sum(ph, gi)
                        if k:
                            low(k - 1)
                    low(per - 1)

            def down(ph):
                for gi, g, r, par, first in groups_of(E, ph):
                    for k in range(PIECES):
                        dve.wait_ge(sem["w_used"], E.at("w_used", gi * PIECES + k + 1))
                        xc = x[:, 4 * g + k, :]
                        v.scalar_tensor_tensor(xc, bank(k), res_scale[:, 4 * g + k:4 * g + k + 1], xc,
                                               ALU.mult, ALU.add).then_inc(sem["x_added"], 1)
                        if k == 1:
                            ada_sum(ph, gi)

            def pool_mix(ph):
                f0 = f_t[:, 0, :]
                v.tensor_scalar(f_t[:, 1, :], f0, lay[0:8, LY["f_bias"]:LY["f_bias"] + 1], None, ALU.add)\
                    .then_inc(sem["forget_dve"], 1)
                for g in range(4):
                    src, n = qk[:, g, :], 0
                    for step in range(g + 1):
                        sh, dst = 2 ** step, pool_s[:, step % 2, :]
                        v.tensor_copy(dst[:, 0:sh], src[:, 0:sh]).then_inc(dve_chain, 1)
                        dve.wait_ge(dve_chain, E.step())
                        v.tensor_tensor(dst[:, sh:S], src[:, sh:S], src[:, 0:S - sh], ALU.add).then_inc(dve_chain, 1)
                        dve.wait_ge(dve_chain, E.step())
                        src = dst
                    w = CS["inv_count"] + 16 * g
                    v.tensor_tensor(src[:, 0:16], src[:, 0:16], cst[:, w:w + 16], ALU.mult).then_inc(dve_chain, 1)
                    dve.wait_ge(dve_chain, E.step())
                    v.tensor_scalar(src[:, 16:S], src[:, 16:S], 1.0 / 2 ** (g + 1), None, ALU.mult).then_inc(dve_chain, 1)
                    dve.wait_ge(dve_chain, E.step())
                    if g:
                        dve.wait_ge(sem["pool_mm"], E.at("pool_mm", g))
                    v.tensor_tensor(pool_d[:], src, qk[:, g, :], ALU.subtract).then_inc(sem["pool_in"], 1)
                    dve.wait_ge(sem["pool_in"], E.at("pool_in", g + 1))
                dve.wait_ge(sem["forget_dve"], E.at("forget_dve", 1))
                v.tensor_scalar(f_t[:, 0, :], f_t[:, 1, :], 0.0, None, ALU.min).then_inc(dve_chain, 1)
                dve.wait_ge(dve_chain, E.step())
                dve.wait_ge(sem["forget_step"], E.at("forget_step", 2))
                v.tensor_tensor(f_t[:, 0, :], f_t[:, 3, :], f_t[:, 0, :], ALU.subtract).then_inc(dve_chain, 1)
                dve.wait_ge(dve_chain, E.step())
                v.memset(f_t[:, 1, :], 1.0).then_inc(dve_chain, 1)
                dve.wait_ge(dve_chain, E.step())
                v.tensor_tensor_scan(f_t[:, 4, :], f_t[:, 1, :], f_t[:, 0, :], 0.0, ALU.mult, ALU.add)\
                    .then_inc(sem["forget_dve"], 2)

            def prep(ph):
                dve.wait_ge(sem["prep_loaded"], E.at("prep_loaded", 80))
                for n in (0, 1):
                    v.tensor_tensor_reduce(out=rs_t[:, n, 0:HALF], in0=lam_w[:, 2 * n, :],
                                           in1=lam_w[:, 2 * n + 1, :], scale=1.0, scalar=0.0, op0=ALU.mult,
                                           op1=ALU.add, accum_out=lam_t[:, n:n + 1]).then_inc(sem["prep_step"], 1)
                v.tensor_copy(ident_16[:], ident).then_inc(dve_chain, 1)
                dve.wait_ge(dve_chain, E.step())
                v.tensor_copy(tri_16[:], cst[:, CS["tri"]:CS["tri"] + P]).then_inc(dve_chain, 1)
                dve.wait_ge(dve_chain, E.step())
                dve.wait_ge(sem["prep_step"], E.at("prep_step", 4))
                v.tensor_tensor(neg_lam[:], lam_t[:, 3:4], lam_t[:, 2:3], ALU.subtract).then_inc(dve_chain, 1)
                dve.wait_ge(dve_chain, E.step())
                v.tensor_scalar(neg_lam[:], neg_lam[:], -LAM_INIT, None, ALU.add).then_inc(dve_chain, 1)
                dve.wait_ge(dve_chain, E.step())

            def run(ph):
                kind = ph.kind
                if kind == "prep":
                    prep(ph)
                elif kind == "norm":
                    norm(ph)
                elif kind.startswith("proj"):
                    proj(ph)
                elif kind.startswith("att"):
                    attention(ph)
                elif kind == "compress":
                    compress(ph)
                elif kind.startswith("split"):
                    split(ph)
                elif kind == "merge":
                    merge(ph)
                elif kind == "msplit":
                    msplit(ph)
                elif kind.endswith("up"):
                    up(ph)
                elif kind == "down":
                    down(ph)
                elif kind == "pool":
                    pool_mix(ph)
                elif kind == "layer":
                    dve.wait_ge(sem["layer_loaded"], E.at("layer_loaded", 32))
                    dve.nop(nofuse=True)
                    v.tensor_copy(mod[:, 0:3 * KC], mods[:, bass.ds(E.turn * (3 * KC), 3 * KC)]).then_inc(dve_chain, 1)
                    dve.wait_ge(dve_chain, E.step())
                    v.tensor_tensor(mod[:, 0:3 * KC], mod[:, 0:3 * KC], col(lay, LY["b_ada"], 3 * KC), ALU.add)\
                        .then_inc(dve_chain, 1)
                    dve.wait_ge(dve_chain, E.step())
                if not ph.meets:
                    return
                dve.nop(nofuse=True)
                dve.drain().then_inc(sem["phase_done"], 1)
                dve.wait_ge(sem["phase_done"], E.at("phase_done", 3))

            walk(E, run)


def tiles_of(w):
    k, n = w.shape
    return w.reshape(k // P, P, n).transpose(1, 0, 2).reshape(P, -1)


def stream(groups):
    return np.concatenate([np.concatenate(g, axis=1).ravel() for g in groups])


def blocks_of(w, n):
    return [tiles_of(w[:, P * i:P * (i + 1)]) for i in range(n)]


def fours(blocks):
    return [blocks[i:i + 4] for i in range(0, len(blocks), 4)]


def mix_groups(w_gate, w_branch, w_out):
    out = [[tiles_of(w_gate[:, n * D + d * P:n * D + (d + 1) * P]), tiles_of(w_branch[n][:, d * P:(d + 1) * P])]
           for d in range(KC) for n in range(3)]
    return out + fours(blocks_of(w_out, KC))


def bucket(dist):
    n = np.maximum(dist, 0)
    large = 16 + (np.log(np.maximum(n, 1).astype(np.float32) / np.float32(16)) / np.float32(np.log(8.0))
                  * np.float32(16)).astype(np.int32)
    return np.where(n < 16, n, np.minimum(large, 31))


def kernel(x, w_in, qk_gain, diff_lambda, diff_subln, sinks, cmp_pos, cmp_w1, cmp_w2, w_branch, w_out,
           norm_mix, norm_mlp, w_up, w_down, rel_bias, c_2, w_ada_2, b_ada_2, norm_gain_2,
           ffn_w_gate_2, ffn_w_up_2, ffn_w_down_2, w_in_2, qk_gain_2, rel_bias_2, forget_bias_2,
           w_pool_2, pool_scale_2, w_branch_2, w_out_2):
    import concourse.bacc as bacc
    from concourse.bass_utils import run_bass_kernel_spmd

    arr = np.ascontiguousarray
    (x, w_in, qk_gain, diff_lambda, diff_subln, sinks, cmp_pos, cmp_w1, cmp_w2, w_branch, w_out, norm_mix,
     norm_mlp, w_up, w_down, rel_bias, c_2, w_ada_2, b_ada_2, norm_gain_2, ffn_w_gate_2, ffn_w_up_2,
     ffn_w_down_2, w_in_2, qk_gain_2, rel_bias_2, forget_bias_2, w_pool_2, pool_scale_2, w_branch_2,
     w_out_2) = map(np.asarray, (
         x, w_in, qk_gain, diff_lambda, diff_subln, sinks, cmp_pos, cmp_w1, cmp_w2, w_branch, w_out,
         norm_mix, norm_mlp, w_up, w_down, rel_bias, c_2, w_ada_2, b_ada_2, norm_gain_2, ffn_w_gate_2,
         ffn_w_up_2, ffn_w_down_2, w_in_2, qk_gain_2, rel_bias_2, forget_bias_2, w_pool_2,
         pool_scale_2, w_branch_2, w_out_2))

    heads = np.array([g * 4 + r for r in range(4) for g in range(2)])
    by_pair = (heads[:, None] * HALF + np.arange(HALF)).ravel()
    w = w_in[0]
    ends = np.cumsum([512, 512, 512, 512, 128, 128, 512, 768, 24, 3072])
    aq, ak, av, bq, bk, bv, cq, ckv, cg, mg = np.split(w, ends[:-1], axis=1)
    ck = [ckv[:, i * P:(i + 1) * P] for i in range(6)]
    cg = cg.reshape(D, 8, 3)[:, heads].reshape(D, GATES)
    wb = [w_branch[0, 0], w_branch[0, 1][by_pair], w_branch[0, 2][by_pair]]
    first = [blocks_of(aq, 4), blocks_of(ak, 4), [tiles_of(av)],
             blocks_of(bq[:, by_pair], 4), [tiles_of(t) for t in (bk, ck[2], ck[4], ck[0])], [tiles_of(ck[1])],
             [tiles_of(np.concatenate([bv, ck[3], ck[5], cg], axis=1))],
             blocks_of(cq[:, by_pair], 4)] + mix_groups(mg, wb, w_out[0])
    mlp = []
    for m in range(4):
        part = slice(m * D, (m + 1) * D)
        mlp += fours(blocks_of(w_up[0][:, part], 8)) + fours(blocks_of(w_down[0][part], 8))

    def ffn(l, n):
        out, at = [], 0
        for chunks in FFN_PARTS:
            part = slice(at * P, (at + chunks) * P)
            gate, up = (blocks_of(t[l, n][:, part], chunks) for t in (ffn_w_gate_2, ffn_w_up_2))
            out += [[gate[i], up[i], gate[i + 1], up[i + 1]] for i in range(0, chunks, 2)]
            out += fours(blocks_of(ffn_w_down_2[l, n][part], 8))
            at += chunks
        return out

    layers = []
    for l in range(2):
        qa, ka, va, ub, qc, kc, vc, f, g = np.split(w_in_2[l], np.cumsum([512] * 7 + [8]), axis=1)
        f = np.concatenate([f, np.zeros((D, P - 8), f.dtype)], axis=1)
        layers += ffn(l, 0) + [blocks_of(qa, 4), blocks_of(ka, 4), [tiles_of(va)], blocks_of(ub, 4),
                               [tiles_of(f)], blocks_of(qc, 4), blocks_of(kc, 4), [tiles_of(vc)]]
        layers += mix_groups(g, w_branch_2[l], w_out_2[l]) + ffn(l, 1)

    def cols(v):
        return v.reshape(-1, P).T

    def both(v):
        return np.concatenate([v.T, v.T], axis=0)

    pos = cmp_pos[0].reshape(2, CMP_STRIDE, 2, HALF).transpose(2, 3, 0, 1).reshape(P, 2 * CMP_STRIDE)
    w2 = cmp_w2[0].reshape(2, 2, P, HALF).transpose(2, 0, 1, 3).reshape(P, 4 * HALF)
    small = np.concatenate([cols(norm_mix[0]), cols(norm_mlp[0]), both(qk_gain[0]), diff_subln[0][:, None],
                            np.broadcast_to(sinks[0][heads], (P, 8)), pos, w2], axis=1)
    lay = []
    for l in range(2):
        fb = np.concatenate([forget_bias_2[l], np.zeros(P - 8, np.float32)])[:, None]
        lay.append(np.concatenate([cols(norm_gain_2[l].ravel()), cols(b_ada_2[l]),
                                   w_pool_2[l].transpose(1, 0, 2).reshape(P, 4 * P), cols(pool_scale_2[l]),
                                   both(qk_gain_2[l]), fb], axis=1))
    dist = 384 + np.arange(P)[:, None] - np.arange(S)[None, :]
    b1 = rel_bias[bucket(dist)].transpose(2, 0, 1)
    b1 = b1[np.concatenate([np.arange(4), 4 + heads, 12 + heads])]
    b2 = rel_bias_2[:, :, np.clip(dist, -128, 128) + 128].reshape(16, P, S)
    w1 = cmp_w1[0].reshape(2, CMP_STRIDE, P, 2 * P).transpose(0, 2, 1, 3)
    ada = w_ada_2.transpose(0, 2, 1).reshape(2, 24, ADA, P, D).transpose(0, 1, 3, 2, 4).reshape(2, 24, P, ADA * D)
    ada = np.concatenate([ada[0, :8], ada[1, :8], ada[0, 8:], ada[1, 8:]])

    i, j = np.arange(P)[:, None], np.arange(P)[None, :]
    c, t = np.arange(CMP_N)[None, None, :], np.arange(S).reshape(TB, P).T[:, :, None]
    consts = np.concatenate([
        i == j, i // HALF == j // HALF, np.where(j > i, NEG, 0), np.where(j <= i, NEG, 0),
        np.where((i < HALF) & (j >= HALF), NEG, 0),
        np.where(c * CMP_STRIDE + 31 <= t, 0, NEG).reshape(P, TB * CMP_N), i >= 31,
        np.broadcast_to(1.0 / np.minimum(np.arange(16)[None, :] + 1, 2.0 ** np.arange(1, 5)[:, None]).reshape(1, 64),
                        (P, 64))], axis=1).astype(np.float32)

    ins = dict(
        x_in=x[0].T.reshape(KC, P, S).transpose(1, 0, 2), w_first=stream(first), w_mlp=stream(mlp),
        w_layer=stream(layers), ada=ada, first_small=small, layer_small=np.stack(lay),
        biases=np.concatenate([b1, b2]), cmp_w1=w1,
        lam_in=np.broadcast_to(diff_lambda[0], (P, 4, HALF)), c_in=np.broadcast_to(c_2, (P, D)), consts=consts)
    ins = {k: arr(v) for k, v in ins.items()}
    nc = bacc.Bacc("TRN2", target_bir_lowering=False, num_devices=1)
    aps = {k: nc.dram_tensor(k + "_dram", v.shape, F32, kind="ExternalInput").ap() for k, v in ins.items()}
    out = nc.dram_tensor("out_dram", (P, KC, S), F32, kind="ExternalOutput").ap()
    build(nc, *aps.values(), out)
    r = run_bass_kernel_spmd(nc, [{k + "_dram": v for k, v in ins.items()}], core_ids=[0])
    got = r.results[0]["out_dram"]
    return arr(got.transpose(1, 0, 2).reshape(D, S).T)[None]
```
